# Optimizing a Trainium2 kernel written in Bass

```python
import math
import jax, jax.numpy as jnp
from jax import lax
import numpy as np

D_MODEL = 1024
BATCH = 1
SEQ = 512
DEPTH = 2

HEAD_DIM = 64
SB_HEADS = 8
SB_WIDTH = SB_HEADS * HEAD_DIM
SB_BLOCK = 128
LRU_WIDTH = 512
LRU_BLOCKS = 8
LRU_BLOCK_DIM = LRU_WIDTH // LRU_BLOCKS
LRU_C = 8.0
CONV_WIDTH = 4
AB_IN_WIDTH = 3 * SB_WIDTH + 2 * LRU_WIDTH
AB_MIX_WIDTH = SB_WIDTH + LRU_WIDTH
SWA_HEADS = 16
SWA_KV_HEADS = 4
SWA_GROUP = SWA_HEADS // SWA_KV_HEADS
SWA_WINDOW = 128
C_IN_WIDTH = (SWA_HEADS + 2 * SWA_KV_HEADS) * HEAD_DIM
C_MIX_WIDTH = SWA_HEADS * HEAD_DIM
ROPE_THETA = 10000.0
N_EXPERTS = 16
N_GROUPS = 4
GROUP_SIZE = N_EXPERTS // N_GROUPS
TOP_K = 2
D_FF = 512
PLE_DIM = 256
N_EVEN = (DEPTH + 1) // 2
N_ODD = DEPTH // 2
DEEPNORM_ALPHA = (2 * DEPTH) ** 0.25
DEEPNORM_BETA = (8 * DEPTH) ** -0.25
LN_EPS = 1e-5

kernel_name = "hybrid_sb_lru_swa_grouped_moe_deepnorm"

def layer_norm(x, g, b):
    xf = x.astype(jnp.float32)
    mu = jnp.mean(xf, axis=-1, keepdims=True)
    var = jnp.mean(jnp.square(xf - mu), axis=-1, keepdims=True)
    y = (xf - mu) * lax.rsqrt(var + LN_EPS) * g.astype(jnp.float32) + b.astype(jnp.float32)
    return y.astype(x.dtype)

def stick_breaking_attention(q, k, v):
    b, s = q.shape[0], q.shape[1]
    n_blk = s // SB_BLOCK
    qb = (q * (HEAD_DIM ** -0.5)).reshape(b, n_blk, SB_BLOCK, SB_HEADS, HEAD_DIM).transpose(1, 0, 3, 2, 4)
    kh = k.transpose(0, 2, 1, 3)
    vh = v.transpose(0, 2, 1, 3)
    key_idx = jnp.arange(s)

    def one_block(args):
        q_blk, blk = args
        z = jnp.einsum('bhqd,bhkd->bhqk', q_blk, kh, preferred_element_type=jnp.float32)
        q_idx = blk * SB_BLOCK + jnp.arange(SB_BLOCK)
        causal = key_idx[None, :] < q_idx[:, None]
        log_keep = jnp.where(causal, -jax.nn.softplus(z), 0.0)
        after = lax.cumsum(log_keep, axis=3, reverse=True) - log_keep
        w = jnp.where(causal, jnp.exp(jax.nn.log_sigmoid(z) + after), 0.0)
        return jnp.einsum('bhqk,bhkd->bqhd', w.astype(vh.dtype), vh)

    out = lax.map(one_block, (qb, jnp.arange(n_blk)))
    return out.transpose(1, 0, 2, 3, 4).reshape(b, s, SB_WIDTH)

def causal_depthwise_conv(x, w, bias):
    y = lax.conv_general_dilated(
        x, w[:, None, :].astype(x.dtype), window_strides=(1,),
        padding=[(CONV_WIDTH - 1, 0)], dimension_numbers=('NWC', 'WIO', 'NWC'),
        feature_group_count=x.shape[-1])
    return y + bias.astype(x.dtype)

def rg_lru(x, w_r, b_r, w_i, b_i, lam):
    b, s, _ = x.shape
    xb = x.reshape(b, s, LRU_BLOCKS, LRU_BLOCK_DIM)
    gate_r = jnp.einsum('bsnc,ncd->bsnd', xb, w_r).reshape(b, s, LRU_WIDTH) + b_r
    gate_i = jnp.einsum('bsnc,ncd->bsnd', xb, w_i).reshape(b, s, LRU_WIDTH) + b_i
    r = jax.nn.sigmoid(gate_r.astype(jnp.float32))
    i = jax.nn.sigmoid(gate_i.astype(jnp.float32))
    log_a = -LRU_C * r * jax.nn.softplus(-lam.astype(jnp.float32))
    a = jnp.exp(log_a)
    u = jnp.sqrt(-jnp.expm1(2.0 * log_a)) * (i * x.astype(jnp.float32))

    def combine(left, right):
        a_l, u_l = left
        a_r, u_r = right
        return a_l * a_r, a_r * u_l + u_r

    _, h = lax.associative_scan(combine, (a, u), axis=1)
    return h.astype(x.dtype)

def mixer_sb_lru(x, w_in, w_out, conv_w, conv_b, w_r, b_r, w_i, b_i, lam):
    b, s, _ = x.shape
    proj = x @ w_in
    q, k, v, xr, gr = jnp.split(
        proj, [SB_WIDTH, 2 * SB_WIDTH, 3 * SB_WIDTH, 3 * SB_WIDTH + LRU_WIDTH], axis=-1)
    heads = lambda t: t.reshape(b, s, SB_HEADS, HEAD_DIM)
    y_sb = stick_breaking_attention(heads(q), heads(k), heads(v))
    h = rg_lru(causal_depthwise_conv(xr, conv_w, conv_b), w_r, b_r, w_i, b_i, lam)
    y_lru = jax.nn.gelu(gr) * h
    return jnp.concatenate([y_sb, y_lru], axis=-1) @ w_out

def rope(x, positions):
    half = HEAD_DIM // 2
    inv_freq = ROPE_THETA ** (-jnp.arange(half, dtype=jnp.float32) / half)
    ang = positions.astype(jnp.float32)[..., None] * inv_freq
    cos = jnp.cos(ang)[:, :, None, :]
    sin = jnp.sin(ang)[:, :, None, :]
    x1 = x[..., :half].astype(jnp.float32)
    x2 = x[..., half:].astype(jnp.float32)
    return jnp.concatenate([x1 * cos - x2 * sin, x2 * cos + x1 * sin], axis=-1).astype(x.dtype)

def sliding_window_attention_with_sinks(q, k, v, sinks):
    b, s = q.shape[0], q.shape[1]
    n_blk = s // SWA_WINDOW
    qb = q.reshape(b, n_blk, SWA_WINDOW, SWA_KV_HEADS, SWA_GROUP, HEAD_DIM)

    def with_prev(t):
        tb = t.reshape(b, n_blk, SWA_WINDOW, SWA_KV_HEADS, HEAD_DIM)
        prev = jnp.pad(tb[:, :-1], ((0, 0), (1, 0), (0, 0), (0, 0), (0, 0)))
        return jnp.concatenate([prev, tb], axis=2)

    kk, vv = with_prev(k), with_prev(v)
    scores = jnp.einsum('bnqkgd,bnskd->bnkgqs', qb, kk,
                        preferred_element_type=jnp.float32) * (HEAD_DIM ** -0.5)
    qi = jnp.arange(SWA_WINDOW)[:, None] + SWA_WINDOW
    si = jnp.arange(2 * SWA_WINDOW)[None, :]
    dist = qi - si
    band = (dist >= 0) & (dist < SWA_WINDOW)
    not_pad = (jnp.arange(n_blk)[:, None, None] > 0) | (si[None] >= SWA_WINDOW)
    mask = band[None] & not_pad
    scores = jnp.where(mask[None, :, None, None], scores, -jnp.inf)
    sink = jnp.broadcast_to(
        sinks.astype(jnp.float32).reshape(SWA_KV_HEADS, SWA_GROUP)[None, None, :, :, None, None],
        scores.shape[:-1] + (1,))
    probs = jax.nn.softmax(jnp.concatenate([scores, sink], axis=-1), axis=-1)[..., :-1]
    out = jnp.einsum('bnkgqs,bnskd->bnqkgd', probs.astype(vv.dtype), vv)
    return out.reshape(b, s, C_MIX_WIDTH)

def mixer_swa(x, positions, w_qkv, w_out, sinks):
    b, s, _ = x.shape
    proj = x @ w_qkv
    q, k, v = jnp.split(proj, [SWA_HEADS * HEAD_DIM, (SWA_HEADS + SWA_KV_HEADS) * HEAD_DIM], axis=-1)
    q = rope(q.reshape(b, s, SWA_HEADS, HEAD_DIM), positions)
    k = rope(k.reshape(b, s, SWA_KV_HEADS, HEAD_DIM), positions)
    v = v.reshape(b, s, SWA_KV_HEADS, HEAD_DIM)
    return sliding_window_attention_with_sinks(q, k, v, sinks) @ w_out

def grouped_moe(x, w_router, b_router, w_gate, w_up, w_down):
    logits = jnp.einsum('bsd,de->bse', x, w_router,
                        preferred_element_type=jnp.float32) + b_router.astype(jnp.float32)
    probs = jax.nn.softmax(logits, axis=-1)
    grouped = probs.reshape(probs.shape[:-1] + (N_GROUPS, GROUP_SIZE))
    group_score = jnp.sum(lax.top_k(grouped, TOP_K)[0], axis=-1)
    g_sel = jnp.argmax(group_score, axis=-1)
    in_group = jnp.take_along_axis(grouped, g_sel[..., None, None], axis=-2)[..., 0, :]
    top_w, top_i = lax.top_k(in_group, TOP_K)
    top_w = top_w / jnp.sum(top_w, axis=-1, keepdims=True)
    expert_idx = g_sel[..., None] * GROUP_SIZE + top_i
    gates = jnp.sum(jax.nn.one_hot(expert_idx, N_EXPERTS, dtype=jnp.float32) * top_w[..., None], axis=-2)
    hidden = jax.nn.silu(jnp.einsum('bsd,edf->bsef', x, w_gate)) * jnp.einsum('bsd,edf->bsef', x, w_up)
    hidden = hidden * gates[..., None].astype(hidden.dtype)
    return jnp.einsum('bsef,efd->bsd', hidden, w_down).astype(x.dtype)

def per_layer_embedding(x, p_i, w_proj, w_gate, b_gate):
    gate = jax.nn.sigmoid(x @ w_gate + b_gate)
    return x + gate * (p_i @ w_proj)

def setup_inputs(seed: int = 0) -> dict:
    key = jax.random.key(seed)
    ks = jax.random.split(key, 28)

    def nrm(k, shape, scale):
        return jax.random.normal(k, shape, jnp.float32) * scale

    x = nrm(ks[0], (BATCH, SEQ, D_MODEL), 1.0)
    p = nrm(ks[1], (DEPTH, BATCH, SEQ, PLE_DIM), 1.0)
    positions = (jnp.arange(SEQ, dtype=jnp.int32)[None, :]
                 + jax.random.randint(ks[2], (BATCH, 1), 0, 1024, dtype=jnp.int32))
    w_in_ab = nrm(ks[3], (N_EVEN, D_MODEL, AB_IN_WIDTH), D_MODEL ** -0.5)
    w_out_ab = nrm(ks[4], (N_EVEN, AB_MIX_WIDTH, D_MODEL), DEEPNORM_BETA * AB_MIX_WIDTH ** -0.5)
    conv_w = nrm(ks[5], (N_EVEN, CONV_WIDTH, LRU_WIDTH), CONV_WIDTH ** -0.5)
    conv_b = nrm(ks[6], (N_EVEN, LRU_WIDTH), 0.01)
    lru_w_r = nrm(ks[7], (N_EVEN, LRU_BLOCKS, LRU_BLOCK_DIM, LRU_BLOCK_DIM), LRU_BLOCK_DIM ** -0.5)
    lru_b_r = nrm(ks[8], (N_EVEN, LRU_WIDTH), 0.01)
    lru_w_i = nrm(ks[9], (N_EVEN, LRU_BLOCKS, LRU_BLOCK_DIM, LRU_BLOCK_DIM), LRU_BLOCK_DIM ** -0.5)
    lru_b_i = nrm(ks[10], (N_EVEN, LRU_WIDTH), 0.01)
    a_c = jax.random.uniform(ks[11], (N_EVEN, LRU_WIDTH), jnp.float32, 0.9, 0.999)
    a0 = a_c ** (1.0 / LRU_C)
    lru_lambda = jnp.log(a0) - jnp.log1p(-a0)
    w_qkv_c = nrm(ks[12], (N_ODD, D_MODEL, C_IN_WIDTH), D_MODEL ** -0.5)
    w_out_c = nrm(ks[13], (N_ODD, C_MIX_WIDTH, D_MODEL), DEEPNORM_BETA * C_MIX_WIDTH ** -0.5)
    sinks_c = nrm(ks[14], (N_ODD, SWA_HEADS), 0.5)
    ln_mix_g = 1.0 + nrm(ks[15], (DEPTH, D_MODEL), 0.01)
    ln_mix_b = nrm(ks[16], (DEPTH, D_MODEL), 0.01)
    ln_ffn_g = 1.0 + nrm(ks[17], (DEPTH, D_MODEL), 0.01)
    ln_ffn_b = nrm(ks[18], (DEPTH, D_MODEL), 0.01)
    w_router = nrm(ks[19], (D_MODEL, N_EXPERTS), D_MODEL ** -0.5)
    b_router = nrm(ks[20], (N_EXPERTS,), 0.01)
    exp_w_gate = nrm(ks[21], (DEPTH, N_EXPERTS, D_MODEL, D_FF), D_MODEL ** -0.5)
    exp_w_up = nrm(ks[22], (DEPTH, N_EXPERTS, D_MODEL, D_FF), D_MODEL ** -0.5)
    exp_w_down = nrm(ks[23], (DEPTH, N_EXPERTS, D_FF, D_MODEL), DEEPNORM_BETA * D_FF ** -0.5)
    ple_w_proj = nrm(ks[24], (DEPTH, PLE_DIM, D_MODEL), PLE_DIM ** -0.5)
    ple_w_gate = nrm(ks[25], (DEPTH, D_MODEL, D_MODEL), D_MODEL ** -0.5)
    ple_b_gate = nrm(ks[26], (DEPTH, D_MODEL), 0.01)
    return {
        'x': x, 'p': p, 'positions': positions,
        'w_in_ab': w_in_ab, 'w_out_ab': w_out_ab, 'conv_w': conv_w, 'conv_b': conv_b,
        'lru_w_r': lru_w_r, 'lru_b_r': lru_b_r, 'lru_w_i': lru_w_i, 'lru_b_i': lru_b_i,
        'lru_lambda': lru_lambda,
        'w_qkv_c': w_qkv_c, 'w_out_c': w_out_c, 'sinks_c': sinks_c,
        'ln_mix_g': ln_mix_g, 'ln_mix_b': ln_mix_b, 'ln_ffn_g': ln_ffn_g, 'ln_ffn_b': ln_ffn_b,
        'w_router': w_router, 'b_router': b_router,
        'exp_w_gate': exp_w_gate, 'exp_w_up': exp_w_up, 'exp_w_down': exp_w_down,
        'ple_w_proj': ple_w_proj, 'ple_w_gate': ple_w_gate, 'ple_b_gate': ple_b_gate,
    }

def reference(x, p, positions, w_in_ab, w_out_ab, conv_w, conv_b, lru_w_r, lru_b_r, lru_w_i,
              lru_b_i, lru_lambda, w_qkv_c, w_out_c, sinks_c, ln_mix_g, ln_mix_b, ln_ffn_g,
              ln_ffn_b, w_router, b_router, exp_w_gate, exp_w_up, exp_w_down, ple_w_proj,
              ple_w_gate, ple_b_gate):
    for i in range(DEPTH):
        j = i // 2
        if i % 2 == 0:
            h = mixer_sb_lru(x, w_in_ab[j], w_out_ab[j], conv_w[j], conv_b[j], lru_w_r[j],
                             lru_b_r[j], lru_w_i[j], lru_b_i[j], lru_lambda[j])
        else:
            h = mixer_swa(x, positions, w_qkv_c[j], w_out_c[j], sinks_c[j])
        x = layer_norm(DEEPNORM_ALPHA * x + h, ln_mix_g[i], ln_mix_b[i])
        m = grouped_moe(x, w_router, b_router, exp_w_gate[i], exp_w_up[i], exp_w_down[i])
        x = layer_norm(DEEPNORM_ALPHA * x + m, ln_ffn_g[i], ln_ffn_b[i])
        x = per_layer_embedding(x, p[i], ple_w_proj[i], ple_w_gate[i], ple_b_gate[i])
    return x


_drawn_inputs = setup_inputs


def setup_inputs(seed=0):
    import zlib

    import numpy as np

    out = dict(_drawn_inputs(seed))
    spreads = {}
    factors = {'conv_b': 3.708,
     'lru_b_r': 22.951,
     'lru_b_i': 24.102,
     'sinks_c': 44.304,
     'ln_ffn_g': 3.333,
     'ln_ffn_b': 2.762,
     'b_router': 2.969,
     'ple_b_gate': 38.029}
    for name, (base, spread) in spreads.items():
        noise = np.random.default_rng([zlib.crc32(name.encode()), seed]).standard_normal(out[name].shape)
        drawn = base * np.exp(spread * noise) if base else spread * noise
        out[name] = __import__('jax').numpy.asarray(drawn.astype(out[name].dtype))
    for name, factor in factors.items():
        out[name] = (out[name] * factor).astype(out[name].dtype)
    return out
```

```python
import concourse.bass as bass
from concourse import mybir
from contextlib import ExitStack

F32 = mybir.dt.float32
BF16 = mybir.dt.bfloat16
I32 = mybir.dt.int32
ALU = mybir.AluOpType
ACT = mybir.ActivationFunctionType
AX = mybir.AxisListType

P = 128
D = 1024
S = 512
DEPTH = 2
NT = S // P
DC = D // P
HD = 64
SBH = 8
SBW = SBH * HD
LRU = 512
LC = LRU // P
SWA_H, SWA_KV = 16, 4
GRP = SWA_H // SWA_KV
NE, NG, GS = 16, 4, 4
DFF = 512
FC = DFF // P
PLE = 256
ALPHA = (2 * DEPTH) ** 0.25
EPS = 1e-5
NEG = -1e30
SLOTS = 6
SLOT_W = DC * 512
WINDOWS = S // P
L_IN = 0
L_OUT = (5, 61)
L_MOE = (7, 63)
L_PLE = (55, 111)
L_QKV = 58
SEG = {0: 0, 1: 512, 3: 896, 2: 1024}
SEGW = 1280
TR_QKV = 39
UNITS = SWA_KV * NT
TR_SWA = TR_QKV + 3 * NT
PI = 3.14159265
TWO_PI = 6.283185307179586
TURN = (6.28125, 2029 / 2 ** 20, TWO_PI - 6.28125 - 2029 / 2 ** 20)


def trunk(nc, x, p, positions, w_in_ab, w_out_ab, conv_w, conv_b, lru_w_r, lru_b_r, lru_w_i,
          lru_b_i, lru_lambda, w_qkv_c, w_out_c, sinks_c, ln_mix_g, ln_mix_b, ln_ffn_g, ln_ffn_b,
          w_router, b_router, exp_w_gate, exp_w_up, exp_w_down, ple_w_proj, ple_w_gate,
          ple_b_gate, out):
    with ExitStack() as ctx:
        def sb(name, shape, dt=F32):
            return ctx.enter_context(nc.sbuf_tensor(name, shape, dt))

        def sem(name):
            return ctx.enter_context(nc.semaphore(name))

        ring = sb("ring", [P, SLOTS * SLOT_W])
        x_tok = sb("x_tok", [P, NT, D])
        xT = sb("xT", [P, DC, S])
        vec_mix = sb("vec_mix", [P, 2, D])
        w_bd = sb("w_bd", [P, 2, LC, P])
        work = sb("work", [P, 15360])
        ident = sb("ident", [P, P])
        neg_tri = sb("neg_tri", [P, P])
        neg_ones = sb("neg_ones", [P, P])
        band = sb("band", [P, 2 * P])
        cos_t = sb("cos_t", [P, NT, 32])
        sin_t = sb("sin_t", [P, 2, NT, 32])
        w_rt = sb("w_rt", [P, DC, NE])
        b_rt = sb("b_rt", [P, NE])
        sinks = sb("sinks", [P, SWA_H])
        lru_p = sb("lru_p", [P, 8, LC])
        conv_p = sb("conv_p", [P, 4, LC])
        slots_bf = sb("slots_bf", [P, P], BF16)
        stri_bf = sb("stri_bf", [P, P], BF16)
        ones_bf = sb("ones_bf", [P, P], BF16)
        tok_id = sb("tok_id", [P, NT, 2], BF16)
        key4 = sb("key4", [P, 4])
        e_base = sb("e_base", [P, NE])
        mhalf = sb("mhalf", [P, 1])
        route = sb("route", [P, 256])
        mask_bf = sb("mask_bf", [P, NT, NE], BF16)
        idx_i = sb("idx_i", [P, NE], I32)
        pos_i = sb("pos_i", [P, WINDOWS, 2, NT], I32)
        most_i = sb("most_i", [P, 1], I32)
        st = sb("st", [P, NT, 2, 6])
        mv = sb("mv", [P, NT, 2])
        lnp = sb("lnp", [P, NT, 4])
        sm = sb("sm", [P, 4, 24])
        bank = [ctx.enter_context(nc.psum_tensor(f"bank{i}", [P, 512], F32)) for i in range(8)]
        x_dram = [nc.dram_tensor(f"x_rows{i}", [S, D], F32).ap() for i in range(DEPTH)]
        y_dram = [[nc.dram_tensor(f"y_rows{i}_{w}", [NE * P, D], F32).ap() for w in range(WINDOWS)] for i in range(DEPTH)]

        def wk(at, n):
            return work[:, at:at + n]

        def slot(n):
            s = n % SLOTS
            return ring[:, s * SLOT_W:(s + 1) * SLOT_W]

        qT = wk(0, 2048).rearrange("p (c s) -> p c s", c=4)
        kT = wk(2048, 2048).rearrange("p (c s) -> p c s", c=4)
        v0 = wk(4096, 2048).rearrange("p (t n) -> p t n", t=NT)
        gr = wk(6144, 2048).rearrange("p (c s) -> p c s", c=LC)
        xr = wk(8192, 2048).rearrange("p (c s) -> p c s", c=LC)
        xc = wk(10240, 2048).rearrange("p (c s) -> p c s", c=LC)
        gi = wk(12288, 2048).rearrange("p (c s) -> p c s", c=LC)
        r_t = wk(14336, 512)
        r_d = wk(14848, 512)
        rows = work[0:36, 0:P]
        pos_row = work[32:36, P:2 * P].bitcast(I32)
        slot_i = wk(14336, P).bitcast(I32)
        turns_i = wk(14848, P).bitcast(I32).rearrange("p (t f) -> p t f", t=NT)
        zb = [wk(8192 + SEGW * i, SEGW) for i in range(3)]
        xT_flat = xT[:, :, :].rearrange("p c s -> p (c s)")
        tb = [wk(12032, SEGW), xT_flat[:, 2048:2048 + SEGW]]
        y_sb = wk(13312, 2048).rearrange("p (t n) -> p t n", t=NT)
        raw = [wk(1280 * i, 1280) for i in range(2)]
        rope_a, rope_b = wk(2560, 1280), wk(3840, 1280)
        rot = [wk(5120 + 1536 * i, 1536) for i in range(2)]
        qT1 = wk(8192, 4096).rearrange("p (c s) -> p c s", c=8)
        kT1 = wk(12288, 2048).rearrange("p (c s) -> p c s", c=4)
        v1 = wk(14336, 1024).rearrange("p (t n) -> p t n", t=NT)
        sc = [wk(at, 1024).rearrange("p (h s) -> p h s", h=GRP) for at in (0, 1024, 6144)]
        pT1 = [wk(2048 + 1024 * i, 1024).rearrange("p (j n) -> p j n", j=2) for i in range(2)]
        y_sw = [wk(4096 + 1024 * i, 1024) for i in range(2)]
        vec_ffn = wk(0, 2048).rearrange("p (k n) -> p k n", k=2)
        b_ple = wk(2048, 1024)
        p_tok = wk(3072, 1024).rearrange("p (t n) -> p t n", t=NT)
        pT = wk(4096, 1024).rearrange("p (c s) -> p c s", c=2)
        xe = [wk(5120 + 1024 * i, 1024) for i in range(2)]
        xeT = [wk(7168 + 1024 * i, 1024).rearrange("p (c s) -> p c s", c=DC) for i in range(2)]
        hh = [wk(9216 + 512 * i, 512) for i in range(2)]
        hT = [wk(10240 + 512 * i, 512) for i in range(2)]
        th = [wk(11264 + 512 * i, 512) for i in range(2)]
        yy = [wk(12288 + 1024 * i, 1024) for i in range(2)]
        onehot = [wk(10240 + 1024 * t, 1024).bitcast(BF16).rearrange("p (e s) -> p e s", e=NE) for t in range(NT)]
        yg = [wk(5120 + 2048 * i, 2048).rearrange("p (k n) -> p k n", k=2) for i in range(2)]
        gt = [wk(9216 + 512 * i, 512) for i in range(2)]
        r_probs = wk(14336, 64)
        rsel = route[:, 0:64].rearrange("p (t e) -> p t e", t=NT)
        rwin = route[:, 64:128].rearrange("p (t e) -> p t e", t=NT)
        wgt = route[:, 128:136].rearrange("p (k t) -> p k t", k=2)

        s_x = [sem(f"x_loaded{t}") for t in range(NT)]
        s_w0 = sem("first_weights_loaded")
        s_small = sem("small_loaded")
        s_bd = sem("gates_loaded")
        s_vmix = sem("ln_mix_loaded")
        s_vffn = sem("ln_ffn_loaded")
        s_p = sem("p_loaded")
        s_posn = sem("positions_loaded")
        s_posf = sem("positions_cast")
        ring_full = [sem(f"ring_full{i}") for i in range(SLOTS)]
        s_ident = sem("ident_made")
        s_pool = sem("pool_step")
        s_const = sem("consts_made")
        s_dve = sem("dve_step")
        s_act = sem("act_step")
        tr_full = sem("transposed")
        tr_out = sem("transposed_copied")
        proj_full = sem("proj_summed")
        proj_out = sem("proj_copied")
        s_lrup = sem("lru_params_ready")
        s_conv = sem("conv_ready")
        gate_full = sem("lru_gates_summed")
        gate_out = sem("lru_gates_read")
        s_T = sem("lru_tanh_ready")
        s_u2 = sem("lru_u2_ready")
        s_sq = sem("lru_root_ready")
        s_lru = sem("lru_ready")
        z_full = sem("z_summed")
        z_out = sem("z_copied")
        s_neg = sem("neg_abs_ready")
        s_ln1p = sem("log1p_ready")
        s_sp = sem("softplus_ready")
        s_spm = sem("softplus_masked")
        c_full = sem("after_summed")
        s_arg = sem("arg_ready")
        s_w = sem("w_ready")
        s_wm = sem("w_masked")
        y_full = sem("y_summed")
        y_out = sem("y_copied")
        op_full = sem("out_proj_summed")
        op_out = sem("out_proj_added")
        s_ve = sem("ln_var_ready")
        s_rstd = sem("ln_rstd_ready")
        s_nb = sem("ln_bias_ready")
        s_xn = sem("ln_normed")
        s_xg = sem("ln_scaled")
        s_xln = sem("ln_ready")
        s_xd = sem("x_rows_written")
        lg_full = sem("logits_summed")
        s_lg = sem("logits_shifted")
        s_ex = sem("router_exp_ready")
        s_mask = sem("mask_ready")
        rk_full = sem("ranks_summed")
        s_onehot = sem("onehot_ready")
        id_full = sem("table_summed")
        s_idx = sem("table_ready")
        s_most = sem("most_ready")
        xe_full = [sem(f"xe_gathered{i}") for i in range(2)]
        xa_full = sem("xe_low_transposed")
        xa_out = sem("xe_low_copied")
        xb_full = sem("xe_high_transposed")
        xb_out = sem("xe_high_copied")
        g_full = sem("gate_summed")
        u_full = sem("up_summed")
        s_th = sem("tanh_ready")
        s_hg = sem("silu_ready")
        s_h = sem("hidden_ready")
        ht_full = sem("hidden_transposed")
        ht_out = sem("hidden_copied")
        ye_full = sem("expert_out_summed")
        ye_out = sem("expert_out_copied")
        y_wr = [sem(f"y_rows_written{i}") for i in range(2)]
        s_yg = [sem(f"y_rows_gathered{i}") for i in range(2)]
        s_y1 = sem("y1_scaled")
        s_comb = sem("combined")
        pg_full = sem("ple_gate_summed")
        s_pg = sem("ple_gate_biased")
        s_pt = sem("ple_tanh_ready")
        s_pp = sem("ple_proj_read")
        s_px = sem("ple_added")
        s_ang = sem("angles_ready")
        s_rope = sem("rope_tables_ready")
        qkv_full = sem("qkv_summed")
        qkv_out = sem("qkv_copied")
        s_ropeb = sem("rope_swapped")
        s_ropea = sem("rope_direct_used")
        s_rot = sem("rotated")
        sc_full = sem("scores_summed")
        sc_out = sem("scores_masked")
        s_nm = sem("max_ready")
        s_pr = sem("probs_ready")
        pt_full = sem("probs_transposed")
        pt_prev = sem("probs_prev_copied")
        pt_cur = sem("probs_cur_copied")
        pv_full = sem("pv_summed")
        pv_out = sem("pv_normed")
        s_out = sem("out_written")
        ov = {(i, w): [sem(f"ov_{n}_{i}_{w}") for n in ("enter", "loaded", "step", "written", "dve", "y_gathered", "x_gathered")]
              for i in range(DEPTH) for w in range(1, WINDOWS)}

        block = ctx.enter_context(nc.Block())

        def wait(eng, s, v):
            if not (isinstance(v, int) and v <= 0):
                eng.wait_ge(s, v)

        def overflow(eng, i, body, stored=()):
            eng.wait_ge(s_most, i + 1)
            most = eng.value_load(most_i[0:1, 0:1], min_val=0, max_val=S)
            for w in range(1, WINDOWS):
                with eng.If(most > w * P):
                    enter = ov[i, w][0]
                    for s in stored:
                        eng.wait_ge(s, 16 * (NE // 2) * (i + 1))
                    eng.drain().then_inc(enter, 1)
                    eng.wait_ge(enter, 5)
                    body(i, w)
            return most

        OV_ROUTE = 3
        OV = 10
        OV_NAMES = ("xeT", "xeT_out", "gu", "tanh", "silu", "h", "hT", "hT_out", "y", "y_out")
        at = {n: OV_ROUTE + k + 1 for k, n in enumerate(OV_NAMES)}

        @block.sync
        def _(sp):
            for t in range(NT):
                sp.dma_start(x_tok[:, t, :], x[0, t * P:(t + 1) * P, :]).then_inc(s_x[t], 16)
            sp.wait_ge(s_posn, 16)
            sp.wait_ge(s_small, 16 * 5)

            def last_use(n):
                for i in range(DEPTH):
                    if L_OUT[i] <= n < L_OUT[i] + 2:
                        return op_full, 8 * i + 7 + n - L_OUT[i]
                    if L_MOE[i] <= n < L_MOE[i] + 3 * NE:
                        e, k = divmod(n - L_MOE[i], 3)
                        return (g_full, u_full, ye_full)[k], (NE * i + e + 1) * (2 if k == 2 else 1)
                    if L_PLE[i] <= n < L_PLE[i] + 3:
                        return pg_full, 8 * i + min(7 + n - L_PLE[i], 8)
                if L_QKV <= n < L_QKV + 3:
                    return qkv_full, 3 * (NT - 1) + n - L_QKV + 1
                return proj_full, 4 * (n - L_IN + 1)

            def load(n, src, j=0, e_dst=None):
                if n >= SLOTS:
                    s, v = last_use(n - SLOTS)
                    if not isinstance(j, int):
                        v = (4 if s is ye_full else 2) * j + v
                    sp.wait_ge(s, v)
                dst = slot(n)[:, 0:e_dst] if e_dst else slot(n)
                sp.dma_start(dst.rearrange("p (c n) -> p c n", c=src.shape[1]), src)\
                  .then_inc(ring_full[n % SLOTS], 16)

            def cols(w, a):
                return w[:, a:a + 512].rearrange("(p c) n -> p c n", c=DC)

            def out_cols(w, a):
                return w[:, a:a + 512].rearrange("(c p) n -> p c n", c=DC)

            def experts(i):
                def expert_src(e):
                    sel = (lambda w: w[i, e]) if isinstance(e, int) else \
                          (lambda w: w[i, bass.ds(e, 1)].rearrange("o k n -> (o k) n"))
                    return (sel(exp_w_gate).rearrange("(p c) n -> p c n", c=DC),
                            sel(exp_w_up).rearrange("(p c) n -> p c n", c=DC),
                            sel(exp_w_down).rearrange("(p c) n -> p c n", c=FC))
                return expert_src

            def moe(i):
                src = experts(i)
                for e in range(2):
                    for k, s in enumerate(src(e)):
                        load(L_MOE[i] + 3 * e + k, s)
                with sp.Fori(0, NE // 2 - 1) as j:
                    for b in range(2, 4):
                        for k, s in enumerate(src(2 * j + b)):
                            load(L_MOE[i] + 3 * b + k, s, j)

                def window(i, w):
                    _, loaded, step = ov[i, w][:3]
                    own = L_PLE[i] + 3
                    for k in range(3):
                        sp.dma_start(slot(own + k), src(0)[k].rearrange("p c n -> p (c n)")).then_inc(loaded, 16)
                    with sp.Fori(1, NE) as e:
                        sp.wait_ge(step, OV * e + OV_ROUTE)
                        for k, s in enumerate(src(e)):
                            sp.dma_start(slot(own + k), s.rearrange("p c n -> p (c n)")).then_inc(loaded, 16)
                    sp.wait_ge(step, OV * NE + OV_ROUTE)
                return window

            for j in range(4):
                w = w_in_ab[0][:, 1536 + j * P:1536 + (j + 1) * P].rearrange("(p c) n -> p c n", c=DC)
                sp.dma_start(slot(L_IN).rearrange("p (c n) -> p c n", c=DC)[:, :, j * P:(j + 1) * P], w)\
                  .then_inc(s_w0 if j < 3 else ring_full[L_IN], 16)
            for k, a in enumerate((2048, 0, 512, 1024)):
                load(L_IN + 1 + k, cols(w_in_ab[0], a))
            for i in range(DEPTH):
                if i == 1:
                    for s in s_yg:
                        sp.wait_ge(s, 32 * 2)
                    for k in range(3):
                        load(L_QKV + k, cols(w_qkv_c[0], 512 * k))
                for k in range(2):
                    load(L_OUT[i] + k, out_cols((w_out_ab, w_out_c)[i][0], 512 * k))
                window = moe(i)
                for k in range(2):
                    load(L_PLE[i] + k, cols(ple_w_gate[i], 512 * k))
                load(L_PLE[i] + 2, ple_w_proj[i].rearrange("(c p) n -> p c n", c=2), e_dst=2048)
                overflow(sp, i, window)

        @block.tensor
        def _(pe):
            mm, tr = nc.tensor.matmul, nc.tensor.transpose
            n_tr = [0]

            def weights(n, j=0):
                pe.wait_ge(ring_full[n % SLOTS], 16 * (n // SLOTS + 1 + j) if isinstance(j, int) else 16 * j + 16 * (n // SLOTS + 1))
                return slot(n).rearrange("p (c n) -> p c n", n=512)

            def turn4(src):
                n = n_tr[0]
                wait(pe, tr_out, n - 1)
                for k in range(4):
                    last = tr(bank[n % 2][:, k * P:(k + 1) * P], src(k), ident[:, :])
                last.then_inc(tr_full, 1)
                n_tr[0] += 1

            def turn_x(t):
                for a in range(2):
                    turn4(lambda k: x_tok[:, t, 4 * a + k::DC])

            def xT_ready():
                pe.wait_ge(tr_out, n_tr[0])

            pe.wait_ge(s_ident, 1)
            pe.wait_ge(s_small, 16 * 5)
            pe.wait_ge(s_posf, 1)
            tr(bank[0][:, 0:36], rows, ident[0:36, 0:36]).then_inc(tr_full, 1)
            n_tr[0] += 1
            for t in range(NT):
                pe.wait_ge(s_x[t], 16)
                turn_x(t)
            xT_ready()

            for n in range(20):
                kind, j = n // 4, n % 4
                if n < 3:
                    pe.wait_ge(s_w0, 16 * 3)
                    w = slot(L_IN).rearrange("p (c n) -> p c n", n=512)
                else:
                    w = weights(L_IN + kind)
                o = bank[2 + n % 4]
                wait(pe, proj_out, n - 3)
                for c in range(DC):
                    if kind < 4:
                        last = mm(o[:, :], w[:, c, j * P:(j + 1) * P], xT[:, c, :], start=c == 0, stop=c == DC - 1)
                    else:
                        last = mm(o[:, :], xT[:, c, j * P:(j + 1) * P], w[:, c, :], start=c == 0, stop=c == DC - 1)
                last.then_inc(proj_full, 1)
                if 8 <= n < 8 + LC:
                    c = n - 8
                    if c == 0:
                        pe.wait_ge(s_bd, 16 * 7)
                        pe.wait_ge(s_const, 3)
                    pe.wait_ge(s_conv, c + 1)
                    for k in range(2):
                        wait(pe, gate_out, 2 * c - 1 + k)
                        mm(bank[6 + k][:, :], w_bd[:, k, c, :], xc[:, c, :], start=True, stop=True).then_inc(gate_full, 1)

            def z_scores(h):
                r, c = HD * (h % 2), h // 2
                wait(pe, z_out, h)
                for kt in (0, 1, 3, 2):
                    o = SEG[kt]
                    b, o = bank[2 + o // 512], o % 512
                    last = mm(b[:, o:o + S - kt * P], kT[r:r + HD, c, kt * P:(kt + 1) * P], qT[r:r + HD, c, kt * P:S],
                              start=True, stop=True)
                last.then_inc(z_full, 1)

            def after_sums(h):
                pe.wait_ge(s_spm, h + 1)
                wait(pe, s_arg, h)
                t = tb[h % 2]
                for kt in (0, 1, 3, 2):
                    b, o = bank[5 + SEG[kt] // 512], SEG[kt] % 512
                    for k2 in range(kt, NT):
                        width = S - k2 * P
                        last = mm(b[:, o + (k2 - kt) * P:o + (k2 - kt) * P + width],
                                  (neg_tri if k2 == kt else neg_ones)[:, :], t[:, SEG[k2]:SEG[k2] + width],
                                  start=k2 == kt, stop=k2 == NT - 1)
                last.then_inc(c_full, 1)

            def weigh(h):
                pe.wait_ge(s_wm, h + 1)
                wait(pe, y_out, h - 1)
                for qt in range(NT):
                    for kt in range(qt + 1):
                        o = SEG[kt] + (qt - kt) * P
                        last = mm(bank[h % 2][:, qt * HD:(qt + 1) * HD], zb[h % 3][:, o:o + P],
                                  v0[:, kt, h * HD:(h + 1) * HD], start=kt == 0, stop=kt == qt)
                last.then_inc(y_full, 1)

            pe.wait_ge(proj_out, 20)
            z_scores(0)
            for h in range(SBH + 1):
                if h + 1 < SBH:
                    z_scores(h + 1)
                if h < SBH:
                    after_sums(h)
                if h >= 1:
                    weigh(h - 1)
            pe.wait_ge(y_out, SBH)
            for t in range(NT):
                turn4(lambda k: y_sb[:, t, k * P:(k + 1) * P])

            def out_proj(i, t):
                for n in range(2):
                    K = 8 * i + 2 * t + n
                    w = weights(L_OUT[i] + n)
                    wait(pe, op_out, K - 3)
                    for c in range(DC):
                        src = gr[:, c - 4, :] if i == 0 and c >= 4 else xT[:, c, :]
                        last = mm(bank[2 + K % 4][:, :], src[:, t * P:(t + 1) * P], w[:, c, :], start=c == 0, stop=c == DC - 1)
                    last.then_inc(op_full, 1)

            def turn_normed(i, kind, t):
                pe.wait_ge(s_xln, 4 * (2 * i + kind) + t + 1)
                turn_x(t)

            def logits(i, t):
                for c in range(DC):
                    last = mm(bank[6][:, t * NE:(t + 1) * NE], xT[:, c, t * P:(t + 1) * P], w_rt[:, c, :],
                              start=c == 0, stop=c == DC - 1)
                if t == NT - 1:
                    last.then_inc(lg_full, 1)

            def out_and_turn(i):
                for t in range(NT + 2):
                    if t < NT:
                        out_proj(i, t)
                    if t >= 2:
                        xT_ready()
                        logits(i, t - 2)
                    if 1 <= t <= NT:
                        turn_normed(i, 0, t - 1)

            def table_sums(done, ready, value):
                pe.wait_ge(ready, value)
                for e in range(NE):
                    for t in range(NT):
                        last = mm(bank[4][:, 2 * e:2 * e + 2], onehot[t][:, e, :], tok_id[:, t, :], start=t == 0, stop=t == NT - 1)
                last.then_inc(done, 1)

            def router(i):
                pe.wait_ge(s_p, 16 * (i + 1))
                for b in range(2):
                    turn4(lambda k: p_tok[:, 2 * b + k % 2, (k // 2) * P:(k // 2 + 1) * P])
                pe.wait_ge(s_mask, i + 1)
                pe.wait_ge(tr_out, n_tr[0])
                for t in range(NT):
                    for t2 in range(t + 1):
                        mm(bank[3][:, t * NE:(t + 1) * NE], (stri_bf if t2 == t else ones_bf)[:, :], mask_bf[:, t2, :],
                           start=t2 == 0, stop=t2 == t)
                for t in range(NT):
                    last = mm(bank[3][:, NT * NE:(NT + 1) * NE], ones_bf[:, :], mask_bf[:, t, :], start=t == 0, stop=t == NT - 1)
                last.then_inc(rk_full, 1)
                table_sums(id_full, s_onehot, i + 1)

            def experts(i):
                N0 = NE * i
                L = L_MOE[i]

                def turn_xe(half, par, E):
                    b = bank[1 - half]
                    for k in range(4):
                        last = tr(b[:, k * P:(k + 1) * P], xe[par][:, 4 * half + k::DC], ident[:, :])
                    last.then_inc((xa_full, xb_full)[half], 1)

                def gate_up(par, E, n, j):
                    pe.wait_ge(xa_out, E + 1)
                    pe.wait_ge(xb_out, E + 1)
                    wait(pe, s_h, E - 1)
                    for k in range(2):
                        w = weights(n + k, j)
                        for c in range(DC):
                            last = mm(bank[2 + 2 * par + k][:, :], xeT[par][:, c, :], w[:, c, :], start=c == 0, stop=c == DC - 1)
                        last.then_inc((g_full, u_full)[k], 1)

                def turn_hidden(par, E):
                    pe.wait_ge(s_h, E + 1)
                    for k in range(FC):
                        last = tr(bank[0][:, k * P:(k + 1) * P], hh[par][:, k::FC], ident[:, :])
                    last.then_inc(ht_full, 1)

                def down(par, E, n, j, half):
                    if half == 0:
                        pe.wait_ge(ht_out, E + 1)
                        weights(n, j)
                    w = slot(n).rearrange("p (c n) -> p c n", n=D)
                    wait(pe, ye_out, 2 * E - 1 + half)
                    for c in range(FC):
                        last = mm(bank[6 + half][:, :], hT[par][:, c * P:(c + 1) * P], w[:, c, half * 512:(half + 1) * 512],
                                  start=c == 0, stop=c == FC - 1)
                    last.then_inc(ye_full, 1)

                def gathered(par, g):
                    pe.wait_ge(xe_full[par], g)

                def step(par, E, n, j, first, last, g):
                    gate_up(par, E, n, j)
                    if not first:
                        turn_hidden(1 - par, E - 1)
                    if not last:
                        gathered(1 - par, g)
                        turn_xe(0, 1 - par, E + 1)
                    if not first:
                        down(1 - par, E - 1, n - 1, j, 0)
                    if not last:
                        turn_xe(1, 1 - par, E + 1)
                    if not first:
                        down(1 - par, E - 1, n - 1, j, 1)

                G0 = 16 * (NE // 2) * i
                gathered(0, G0 + 16)
                turn_xe(0, 0, N0)
                turn_xe(1, 0, N0)
                step(0, N0, L, 0, True, False, G0 + 16)
                step(1, N0 + 1, L + 3, 0, False, False, G0 + 32)
                step(0, N0 + 2, L + 6, 0, False, False, G0 + 32)
                with pe.Fori(1, NE // 2 - 1) as j:
                    step(1, 2 * j + (N0 + 1), L + 3, j, False, False, 16 * j + (G0 + 32))
                    step(0, 2 * j + (N0 + 2), L + 6, j, False, False, 16 * j + (G0 + 32))
                step(1, N0 + NE - 1, L + 3 * (NE - 1), 0, False, True, 0)
                turn_hidden(1, N0 + NE - 1)
                down(1, N0 + NE - 1, L + 3 * NE - 1, 0, 0)
                down(1, N0 + NE - 1, L + 3 * NE - 1, 0, 1)

            def window(i, w):
                _, loaded, step = ov[i, w][:3]
                own = L_PLE[i] + 3
                table_sums(step, step, 1)
                with pe.Fori(0, NE) as e:
                    def before(name):
                        pe.wait_ge(step, OV * e + (at[name] - 1))
                    before("xeT")
                    pe.wait_ge(loaded, 48 * e + 48)
                    pe.wait_ge(ov[i, w][6], 16 * e + 16)
                    for c in range(DC):
                        last = tr(bank[c // 4][:, (c % 4) * P:(c % 4 + 1) * P], xe[0][:, c::DC], ident[:, :])
                    last.then_inc(step, 1)
                    before("gu")
                    for k in range(2):
                        for c in range(DC):
                            last = mm(bank[2 + k][:, :], xeT[0][:, c, :], slot(own + k)[:, c * 512:(c + 1) * 512], start=c == 0, stop=c == DC - 1)
                    last.then_inc(step, 1)
                    before("hT")
                    for c in range(FC):
                        last = tr(bank[0][:, c * P:(c + 1) * P], hh[0][:, c::FC], ident[:, :])
                    last.then_inc(step, 1)
                    before("y")
                    for k in range(2):
                        for c in range(FC):
                            last = mm(bank[6 + k][:, :], hT[0][:, c * P:(c + 1) * P], slot(own + 2)[:, c * D + k * 512:c * D + (k + 1) * 512],
                                      start=c == 0, stop=c == FC - 1)
                    last.then_inc(step, 1)
                pe.wait_ge(step, OV * NE + OV_ROUTE)

            def ple_and_turn(i):
                def gate(t, n):
                    K = 8 * i + 2 * t + n
                    w = weights(L_PLE[i] + n)
                    wait(pe, s_pg, K - 3)
                    for c in range(DC):
                        last = mm(bank[2 + K % 4][:, :], xT[:, c, t * P:(t + 1) * P], w[:, c, :], start=c == 0, stop=c == DC - 1)
                    weights(L_PLE[i] + 2)
                    w = slot(L_PLE[i] + 2)[:, 0:2048].rearrange("p (c n) -> p c n", c=2)
                    wait(pe, s_pp, K - 1)
                    for c in range(2):
                        last = mm(bank[6 + n][:, :], pT[:, c, t * P:(t + 1) * P], w[:, c, n * 512:(n + 1) * 512],
                                  start=c == 0, stop=c == 1)
                    last.then_inc(pg_full, 1)

                turn_normed(i, 1, 0)
                for t in range(NT + 1):
                    if t < NT:
                        xT_ready()
                        gate(t, 0)
                        if t + 1 < NT and t < 1:
                            turn_normed(i, 1, t + 1)
                        gate(t, 1)
                    if 1 <= t < NT - 1:
                        turn_normed(i, 1, t + 1)
                    if i + 1 < DEPTH and t >= 1:
                        pe.wait_ge(s_px, 8 * i + 2 * t)
                        turn_x(t - 1)

            def qkv():
                xT_ready()
                for t in range(NT + 1):
                    if t < NT:
                        for n in range(3):
                            K = 3 * t + n
                            w = weights(L_QKV + n)
                            wait(pe, qkv_out, K - 5)
                            for c in range(DC):
                                last = mm(bank[2 + K % 6][:, :], xT[:, c, t * P:(t + 1) * P], w[:, c, :], start=c == 0, stop=c == DC - 1)
                            last.then_inc(qkv_full, 1)
                    if t >= 1:
                        pe.wait_ge(s_rot, t)
                        for a in range(3):
                            turn4(lambda k: rot[(t - 1) % 2][:, (4 * a + k) * P:(4 * a + k + 1) * P])

            def scores(u):
                b, kv = divmod(u, SWA_KV)
                wait(pe, sc_out, u - 1)
                lo = (b - 1) * P if b else 0
                for g in (0, 2, 1, 3):
                    h = GRP * kv + g
                    r = HD * (h % 2)
                    o = bank[2 + 2 * (u % 2) + g % 2][:, (g // 2) * 256 + (0 if b else P):(g // 2 + 1) * 256]
                    last = mm(o, qT1[r:r + HD, h // 2, b * P:(b + 1) * P], kT1[r:r + HD, kv, lo:(b + 1) * P], start=True, stop=True)
                last.then_inc(sc_full, 1)

            def swa():
                def turn_probs(u):
                    b = u // SWA_KV
                    pe.wait_ge(s_pr, u + 1)
                    pe.wait_ge(tr_out, n_tr[0])
                    wait(pe, pt_cur, u)
                    wait(pe, pt_prev, u - SWA_KV)
                    for j in (0, 1) if b else (1,):
                        for g in range(GRP):
                            last = tr(bank[j][:, g * P:(g + 1) * P], sc[u % 3][:, g, j * P:(j + 1) * P], ident[:, :])
                    last.then_inc(pt_full, 1)

                def weigh_v(u):
                    b, kv = divmod(u, SWA_KV)
                    js = (0, 1) if b else (1,)
                    pe.wait_ge(pt_cur, u + 1)
                    if b:
                        pe.wait_ge(pt_prev, u - SWA_KV + 1)
                    wait(pe, pv_out, u - 1)
                    for g in range(GRP):
                        for j in js:
                            last = mm(bank[6 + u % 2][:, g * HD:(g + 1) * HD], pT1[u % 2][:, j, g * P:(g + 1) * P],
                                      v1[:, b - 1 + j, kv * HD:(kv + 1) * HD], start=j == js[0], stop=j == 1)
                    last.then_inc(pv_full, 1)

                def turn_y(b, u):
                    pe.wait_ge(pv_out, SWA_KV * (b + 1))
                    pe.wait_ge(pt_cur, u)
                    pe.wait_ge(pt_prev, u - SWA_KV)
                    for a in range(2):
                        turn4(lambda k: y_sw[b % 2][:, (4 * a + k) * P:(4 * a + k + 1) * P])

                xT_ready()
                scores(0)
                scores(1)
                for u in range(UNITS + 2):
                    if u + 2 < UNITS:
                        scores(u + 2)
                    if u < UNITS:
                        turn_probs(u)
                    if 1 <= u <= UNITS:
                        weigh_v(u - 1)
                    if u >= 2 and (u - 2) % SWA_KV == SWA_KV - 1:
                        turn_y((u - 2) // SWA_KV, min(u + 1, UNITS))

            for i in range(DEPTH):
                if i == 1:
                    qkv()
                    swa()
                xT_ready()
                if i == 0:
                    pe.wait_ge(s_lru, 1)
                out_and_turn(i)
                router(i)
                experts(i)
                overflow(pe, i, window)
                ple_and_turn(i)

        @block.scalar
        def _(act):
            A = nc.scalar.activation
            n_tr, n_seq = [0], [0]

            def link(inst):
                inst.then_inc(s_act, 1)
                n_seq[0] += 1
                act.wait_ge(s_act, n_seq[0])

            def copy_out(dst, view="p (c s) -> p c s", **kw):
                n = n_tr[0]
                act.wait_ge(tr_full, n + 1)
                A(dst, bank[n % 2][:, :].rearrange(view, **kw), ACT.Copy).then_inc(tr_out, 1)
                n_tr[0] += 1

            def copy_x(t):
                for a in range(2):
                    copy_out(xT[:, 4 * a:4 * a + 4, t * P:(t + 1) * P], c=4)

            act.dma_start(pos_row, positions[0].rearrange("(t p) -> t p", p=P)).then_inc(s_posn, 16)
            for k, v in enumerate((conv_b, lru_b_r, lru_b_i, lru_lambda)):
                act.dma_start(rows[LC * k:LC * k + LC, :], v[0].rearrange("(c p) -> c p", p=P)).then_inc(s_small, 16)
            act.dma_start(rows[16:32, :], conv_w[0].rearrange("w (c p) -> (w c) p", p=P)).then_inc(s_small, 16)
            act.dma_start(vec_mix[:, 0, :], ln_mix_g[0].partition_broadcast(P)).then_inc(s_vmix, 16)
            act.dma_start(vec_mix[:, 1, :], ln_mix_b[0].partition_broadcast(P)).then_inc(s_vmix, 16)
            act.wait_ge(s_const, 1)
            for k, w in enumerate((lru_w_r, lru_w_i)):
                for h in range(2):
                    act.dma_start(w_bd[h * HD:(h + 1) * HD, k, :, h * HD:(h + 1) * HD],
                                  w[0].rearrange("(c h) i o -> h i c o", h=2)[h]).then_inc(s_bd, 16)
            act.dma_start(w_rt[:, :, :], w_router.rearrange("(p c) e -> p c e", c=DC)).then_inc(s_bd, 16)
            act.dma_start(b_rt[:, :], b_router.partition_broadcast(P)).then_inc(s_bd, 16)
            act.dma_start(sinks[:, :], sinks_c[0].partition_broadcast(P)).then_inc(s_bd, 16)

            act.wait_ge(tr_full, 1)
            A(lru_p[:, 0:4, :], bank[0][:, 0:16].rearrange("p (k c) -> p k c", k=4), ACT.Copy)
            A(conv_p[:, :, :], bank[0][:, 16:32].rearrange("p (w c) -> p w c", w=4), ACT.Copy)
            A(route[:, 0:4], bank[0][:, 32:36], ACT.Copy).then_inc(tr_out, 1)
            n_tr[0] += 1
            for t in range(NT):
                copy_x(t)

            act.wait_ge(s_lrup, 1)
            A(lru_p[:, 5, :], lru_p[:, 5, :], ACT.Exp).then_inc(s_lrup, 1)
            act.wait_ge(s_ang, 2)
            A(cos_t[:, :, :], cos_t[:, :, :], ACT.Sin).then_inc(s_rope, 1)
            A(sin_t[:, 1, :, :], sin_t[:, 1, :, :], ACT.Sin).then_inc(s_rope, 1)

            for n in range(20):
                kind, j = n // 4, n % 4
                act.wait_ge(proj_full, n + 1)
                dst = ((xr, gr, qT, kT, v0)[kind])[:, j, :]
                A(dst, bank[2 + n % 4][:, :], ACT.Gelu_apprx_tanh if kind == 1 else ACT.Copy).then_inc(proj_out, 1)
                if n == 15:
                    act.wait_ge(s_u2, LC)
                    A(gi[:, :, :], gi[:, :, :], ACT.Sqrt, scale=-1.0).then_inc(s_sq, 1)
                if 9 <= n < 9 + LC:
                    c = n - 9
                    if c == 0:
                        act.wait_ge(s_lrup, 3)
                    act.wait_ge(gate_full, 2 * c + 1)
                    wait(act, s_u2, c)
                    A(r_t, bank[6][:, :], ACT.Tanh, scale=0.5, bias=lru_p[:, 1, c:c + 1]).then_inc(gate_out, 1)
                    act.wait_ge(gate_full, 2 * c + 2)
                    A(gi[:, c, :], bank[7][:, :], ACT.Tanh, scale=0.5, bias=lru_p[:, 2, c:c + 1]).then_inc(gate_out, 1)
                    act.wait_ge(gate_out, 2 * c + 1)
                    A(r_t, r_t, ACT.Tanh, scale=lru_p[:, 4, c:c + 1], bias=lru_p[:, 4, c:c + 1]).then_inc(s_T, 1)

            def z_copy(h):
                act.wait_ge(z_full, h + 1)
                wait(act, y_full, h - 2)
                for b, (o, n) in enumerate(((0, 512), (512, 512), (1024, 256))):
                    last = A(zb[h % 3][:, o:o + n], bank[2 + b][:, 0:n], ACT.Copy, scale=HD ** -0.5)
                last.then_inc(z_out, 1)

            def log1p_exp(h):
                act.wait_ge(s_neg, h + 1)
                link(A(tb[h % 2], tb[h % 2], ACT.Exp))
                A(tb[h % 2], tb[h % 2], ACT.Ln, bias=1.0).then_inc(s_ln1p, 1)

            act.wait_ge(s_lru, 1)
            z_copy(0)
            log1p_exp(0)
            for h in range(SBH):
                if h + 1 < SBH:
                    z_copy(h + 1)
                    log1p_exp(h + 1)
                act.wait_ge(s_arg, h + 1)
                A(zb[h % 3], zb[h % 3], ACT.Exp).then_inc(s_w, 1)
            for t in range(NT):
                copy_out(xT[:, 0:4, t * P:(t + 1) * P], c=4)

            def normalize(i, kind, t):
                act.wait_ge(s_nb, 4 * (2 * i + kind) + t + 1)
                A(x_tok[:, t, :], x_tok[:, t, :], ACT.Identity, scale=lnp[:, t, 1:2], bias=lnp[:, t, 2:3]).then_inc(s_xn, 1)

            def norm_and_copy(i):
                for t in range(NT + 1):
                    if t < NT:
                        normalize(i, 0, t)
                    if t >= 1:
                        act.wait_ge(s_xln, 8 * i + t)
                        act.dma_start(x_dram[i][(t - 1) * P:t * P, :], x_tok[:, t - 1, :]).then_inc(s_xd, 16)
                        copy_x(t - 1)

            def moe_loads(i):
                act.wait_ge(op_full, 8 * (i + 1))
                act.dma_start(p_tok, p[i, 0].rearrange("(t p) n -> p t n", p=P)).then_inc(s_p, 16)
                act.dma_start(vec_ffn[:, 0, :], ln_ffn_g[i].partition_broadcast(P)).then_inc(s_vffn, 16)
                act.dma_start(vec_ffn[:, 1, :], ln_ffn_b[i].partition_broadcast(P)).then_inc(s_vffn, 16)
                act.dma_start(b_ple, ple_b_gate[i].partition_broadcast(P)).then_inc(s_vffn, 16)
                if i + 1 < DEPTH:
                    act.wait_ge(s_xln, 8 * i + 4)
                    act.dma_start(vec_mix[:, 0, :], ln_mix_g[i + 1].partition_broadcast(P)).then_inc(s_vmix, 16)
                    act.dma_start(vec_mix[:, 1, :], ln_mix_b[i + 1].partition_broadcast(P)).then_inc(s_vmix, 16)

            def router(i):
                act.wait_ge(s_lg, i + 1)
                A(r_probs, r_probs, ACT.Exp).then_inc(s_ex, 1)
                for b in range(2):
                    copy_out(pT[:, :, b * 256:(b + 1) * 256], c=2)

            def experts(i):
                N0 = NE * i

                def tanh(par, E):
                    act.wait_ge(g_full, E + 1)
                    wait(act, s_h, E - 1)
                    A(th[par], bank[2 + 2 * par][:, :], ACT.Tanh, scale=0.5).then_inc(s_th, 1)

                def xe_copy(half, par, E):
                    act.wait_ge((xa_full, xb_full)[half], E + 1)
                    A(xeT[par][:, 4 * half:4 * half + 4, :], bank[1 - half][:, :].rearrange("p (c s) -> p c s", c=4), ACT.Copy)\
                        .then_inc((xa_out, xb_out)[half], 1)

                def y_copy(half, par, E, wr):
                    act.wait_ge(ye_full, 2 * E + 1 + half)
                    if half == 0:
                        wait(act, y_wr[par], wr)
                    A(yy[par][:, half * 512:(half + 1) * 512], bank[6 + half][:, :], ACT.Copy).then_inc(ye_out, 1)

                def y_store(par, e, E):
                    act.wait_ge(ye_out, 2 * E + 2)
                    dst = y_dram[i][0][e * P:(e + 1) * P, :] if isinstance(e, int) else y_dram[i][0][bass.ds(e * P, P), :]
                    act.dma_start(dst, yy[par]).then_inc(y_wr[par], 16)

                def step(par, e, E, first, last, wr):
                    tanh(par, E)
                    if not last:
                        xe_copy(0, 1 - par, E + 1)
                    if not first:
                        y_copy(0, 1 - par, E - 1, wr)
                    if not last:
                        xe_copy(1, 1 - par, E + 1)
                    if not first:
                        y_copy(1, 1 - par, E - 1, wr)
                        y_store(1 - par, e - 1, E - 1)

                W0 = 16 * (NE // 2) * i
                xe_copy(0, 0, N0)
                xe_copy(1, 0, N0)
                step(0, 0, N0, True, False, 0)
                step(1, 1, N0 + 1, False, False, W0)
                step(0, 2, N0 + 2, False, False, W0)
                with act.Fori(1, NE // 2 - 1) as j:
                    step(1, 2 * j + 1, 2 * j + (N0 + 1), False, False, 16 * j + W0)
                    step(0, 2 * j + 2, 2 * j + (N0 + 2), False, False, 16 * j + W0)
                step(1, NE - 1, N0 + NE - 1, False, True, W0 + 16 * (NE // 2 - 1))
                y_copy(0, 1, N0 + NE - 1, W0 + 16 * (NE // 2 - 1))
                y_copy(1, 1, N0 + NE - 1, 0)
                y_store(1, NE - 1, N0 + NE - 1)

            def window(i, w):
                step, written = ov[i, w][2:4]

                def expert(e, peeled):
                    def before(name):
                        act.wait_ge(step, e * OV + (at[name] - 1))
                    before("xeT_out")
                    for k in range(2):
                        last = A(xeT[0][:, 4 * k:4 * k + 4, :], bank[k][:, :].rearrange("p (c s) -> p c s", c=4), ACT.Copy)
                    last.then_inc(step, 1)
                    before("tanh")
                    A(th[0], bank[2][:, :], ACT.Tanh, scale=0.5).then_inc(step, 1)
                    before("y_out")
                    if not peeled:
                        act.wait_ge(written, e * 16)
                    for k in range(2):
                        last = A(yy[0][:, k * 512:(k + 1) * 512], bank[6 + k][:, :], ACT.Copy)
                    last.then_inc(step, 1)
                    act.wait_ge(step, e * OV + at["y_out"])
                    dst = y_dram[i][w][0:P, :] if peeled else y_dram[i][w][bass.ds(e * P, P), :]
                    act.dma_start(dst, yy[0]).then_inc(written, 16)
                expert(0, True)
                with act.Fori(1, NE) as e:
                    expert(e, False)
                act.wait_ge(written, 16 * NE)

            def ple(i):
                def tanh(k):
                    act.wait_ge(s_pg, 8 * i + k + 1)
                    A(gt[k % 2], gt[k % 2], ACT.Tanh, scale=0.5).then_inc(s_pt, 1)

                def after(t):
                    if i + 1 < DEPTH:
                        copy_x(t)
                    else:
                        act.wait_ge(s_px, 8 * i + 2 * t + 2)
                        act.dma_start(out[0, t * P:(t + 1) * P, :], x_tok[:, t, :]).then_inc(s_out, 16)

                def scale_and_norm(t):
                    act.wait_ge(s_yg[t % 2], 32 * (2 * i + t // 2 + 1))
                    A(yg[t % 2][:, 0, :], yg[t % 2][:, 0, :], ACT.Copy, scale=wgt[:, 0, t:t + 1]).then_inc(s_y1, 1)
                    normalize(i, 1, t)

                scale_and_norm(0)
                copy_x(0)
                scale_and_norm(1)
                copy_x(1)
                for t in range(NT):
                    tanh(2 * t)
                    tanh(2 * t + 1)
                    if t + 2 < NT:
                        scale_and_norm(t + 2)
                        copy_x(t + 2)
                    after(t)

            def qkv():
                for t in range(NT + 1):
                    if t < NT:
                        wait(act, s_rot, t - 1)
                        for n in range(3):
                            K = 3 * t + n
                            act.wait_ge(qkv_full, K + 1)
                            b = bank[2 + K % 6]
                            if n < 2:
                                A(raw[t % 2][:, n * 512:(n + 1) * 512], b[:, :], ACT.Copy).then_inc(qkv_out, 1)
                            else:
                                A(raw[t % 2][:, 1024:1280], b[:, 0:256], ACT.Copy)
                                A(v1[:, t, :], b[:, 256:512], ACT.Copy).then_inc(qkv_out, 1)
                    if t >= 1:
                        ts = slice((t - 1) * P, t * P)
                        copy_out(qT1[:, 0:4, ts], c=4)
                        copy_out(qT1[:, 4:8, ts], c=4)
                        copy_out(kT1[:, :, ts], c=4)

            def swa():
                def probs(u):
                    b = u // SWA_KV
                    act.wait_ge(s_nm, u + 1)
                    lo = 0 if b else P
                    m = sm[:, u % 4, :]
                    for g in range(GRP):
                        A(sc[u % 3][:, g, lo:], sc[u % 3][:, g, lo:], ACT.Exp, bias=m[:, 4 + g:5 + g], accum_out=m[:, 8 + g:9 + g])
                    A(m[:, 12:16], m[:, 12:16], ACT.Exp).then_inc(s_pr, 1)

                probs(0)
                probs(1)
                for u in range(UNITS + 2):
                    if u < UNITS:
                        act.wait_ge(pt_full, u + 1)
                        wait(act, pv_full, u - 1)
                        if u >= SWA_KV:
                            A(pT1[u % 2][:, 0, :], bank[0][:, :], ACT.Copy).then_inc(pt_prev, 1)
                        A(pT1[u % 2][:, 1, :], bank[1][:, :], ACT.Copy).then_inc(pt_cur, 1)
                    if u + 2 < UNITS:
                        probs(u + 2)
                    if u >= 2 and (u - 2) % SWA_KV == SWA_KV - 1:
                        b = (u - 2) // SWA_KV
                        for a in range(2):
                            copy_out(xT[:, 4 * a:4 * a + 4, b * P:(b + 1) * P], c=4)

            for i in range(DEPTH):
                if i == 1:
                    qkv()
                    swa()
                norm_and_copy(i)
                moe_loads(i)
                router(i)
                experts(i)
                overflow(act, i, window, y_wr)
                ple(i)
            act.wait_ge(s_out, 16 * NT)

        @block.vector
        def _(dve):
            V = nc.vector
            n_seq = [0]

            def link(inst):
                inst.then_inc(s_dve, 1)
                n_seq[0] += 1
                dve.wait_ge(s_dve, n_seq[0])

            dve.wait_ge(s_posn, 16)
            V.tensor_copy(rows[32:36, :], pos_row).then_inc(s_posf, 1)
            dve.wait_ge(tr_out, 1)
            nl, e, s, q, acc = (lru_p[:, k, :] for k in (3, 5, 6, 7, 4))
            link(V.tensor_scalar(nl, nl, -1.0, None, ALU.mult))
            link(V.scalar_tensor_tensor(e, nl, -1.0, nl, ALU.mult, ALU.min))
            V.tensor_scalar(lru_p[:, 1:3, :], lru_p[:, 1:3, :], 0.5, None, ALU.mult).then_inc(s_lrup, 1)
            dve.wait_ge(s_const, 2)
            pos_f, frq = route[:, 0:4], band[:, 0:32]
            ang = route[:, 64:192].rearrange("p (t f) -> p t f", t=NT)
            link(V.tensor_tensor(ang, pos_f.unsqueeze(2).to_broadcast([P, NT, 32]),
                                 frq.unsqueeze(1).to_broadcast([P, NT, 32]), ALU.mult))
            turns_f = sin_t[:, 0, :, :]
            for dst, quarter in ((cos_t[:, :, :], 0.25), (sin_t[:, 1, :, :], 0.0)):
                link(V.tensor_scalar(dst, ang, 1 / TWO_PI, quarter, ALU.mult, ALU.add))
                link(V.tensor_copy(turns_i, dst))
                link(V.tensor_copy(turns_f, turns_i))
                link(V.scalar_tensor_tensor(dst, turns_f, -TURN[0], ang, ALU.mult, ALU.add))
                for part in TURN[1:]:
                    link(V.scalar_tensor_tensor(dst, turns_f, -part, dst, ALU.mult, ALU.add))
                link(V.tensor_scalar(dst, dst, quarter * TWO_PI, PI, ALU.add, ALU.min))
                V.tensor_scalar(dst, dst, -PI, None, ALU.max).then_inc(s_ang, 1)
            dve.wait_ge(s_lrup, 2)
            link(V.tensor_scalar(s, e, 2.0, None, ALU.add))
            link(V.reciprocal(s, s))
            link(V.tensor_tensor(s, s, e, ALU.mult))
            link(V.tensor_tensor(q, s, s, ALU.mult))
            link(V.tensor_scalar(acc, q, 1 / 17, 1 / 15, ALU.mult, ALU.add))
            for k in (13, 11, 9, 7, 5, 3, 1):
                link(V.tensor_tensor(acc, acc, q, ALU.mult))
                link(V.tensor_scalar(acc, acc, 1 / k, None, ALU.add))
            link(V.tensor_tensor(acc, acc, s, ALU.mult))
            link(V.tensor_scalar(nl, nl, 0.0, 2.0, ALU.max, ALU.mult))
            V.scalar_tensor_tensor(acc, acc, 4.0, nl, ALU.mult, ALU.add).then_inc(s_lrup, 1)

            def conv(c):
                dve.wait_ge(proj_out, c + 1)
                link(V.tensor_scalar(xc[:, c, :], xr[:, c, :], conv_p[:, 3, c:c + 1], lru_p[:, 0, c:c + 1], ALU.mult, ALU.add))
                for d in (1, 2, 3):
                    last = V.scalar_tensor_tensor(xc[:, c, d:], xr[:, c, :S - d], conv_p[:, 3 - d, c:c + 1], xc[:, c, d:], ALU.mult, ALU.add)
                    if d < 3:
                        link(last)
                last.then_inc(s_conv, 1)

            def decay(c):
                dve.wait_ge(s_T, c + 1)
                link(V.tensor_scalar(r_d, r_t, 1.0, None, ALU.add))
                link(V.reciprocal(r_d, r_d))
                link(V.scalar_tensor_tensor(r_t, r_t, 2.0, r_d, ALU.mult, ALU.mult))
                V.tensor_scalar(xr[:, c, :], r_t, -1.0, 1.0, ALU.mult, ALU.add)
                link(V.scalar_tensor_tensor(xc[:, c, :], gi[:, c, :], 1.0, xc[:, c, :], ALU.add, ALU.mult))
                V.scalar_tensor_tensor(gi[:, c, :], r_t, 2.0, r_t, ALU.subtract, ALU.mult).then_inc(s_u2, 1)

            for c in range(LC):
                conv(c)
            for c in range(LC):
                decay(c)
            dve.wait_ge(s_sq, 1)
            link(V.scalar_tensor_tensor(xc[:, :, :], xc[:, :, :], 0.5, gi[:, :, :], ALU.mult, ALU.mult))
            for c in range(LC):
                last = V.tensor_tensor_scan(gi[:, c, :], xr[:, c, :], xc[:, c, :], 0.0, ALU.mult, ALU.add)
            link(last)
            dve.wait_ge(proj_out, 8)
            V.tensor_tensor(gr[:, :, :], gr[:, :, :], gi[:, :, :], ALU.mult).then_inc(s_lru, 1)

            def softplus(h):
                z, t = zb[h % 3], tb[h % 2]
                dve.wait_ge(z_out, h + 1)
                wait(dve, c_full, h - 1)
                V.scalar_tensor_tensor(t, z, -1.0, z, ALU.mult, ALU.min).then_inc(s_neg, 1)
                dve.wait_ge(s_ln1p, h + 1)
                V.scalar_tensor_tensor(t, z, 0.0, t, ALU.max, ALU.add).then_inc(s_sp, 1)

            def argument(h):
                dve.wait_ge(c_full, h + 1)
                for b, (o, n) in enumerate(((0, 512), (512, 512), (1024, 256))):
                    last = V.tensor_tensor(zb[h % 3][:, o:o + n], bank[5 + b][:, 0:n], zb[h % 3][:, o:o + n], ALU.add)
                last.then_inc(s_arg, 1)

            def y_copy(h):
                dve.wait_ge(y_full, h + 1)
                if h == 0:
                    dve.wait_ge(s_lru, 1)
                V.tensor_copy(y_sb[:, :, h * HD:(h + 1) * HD], bank[h % 2][:, 0:NT * HD].rearrange("p (t d) -> p t d", t=NT))\
                 .then_inc(y_out, 1)

            softplus(0)
            for h in range(SBH + 1):
                if h + 1 < SBH:
                    softplus(h + 1)
                if h < SBH:
                    argument(h)
                if h >= 1:
                    y_copy(h - 1)

            def ln_stats(i, kind, t):
                for k in range(2):
                    last = V.bn_stats(st[:, t, k, :], x_tok[:, t, k * 512:(k + 1) * 512])
                link(last)
                link(V.bn_aggr(mv[:, t, :], st[:, t, :, :]))
                V.tensor_scalar(lnp[:, t, 0:1], mv[:, t, 1:2], EPS, None, ALU.add).then_inc(s_ve, 1)

            def ln_bias(i, kind, t):
                dve.wait_ge(s_rstd, 4 * (2 * i + kind) + t + 1)
                V.scalar_tensor_tensor(lnp[:, t, 2:3], mv[:, t, 0:1], -1.0, lnp[:, t, 1:2], ALU.mult, ALU.mult).then_inc(s_nb, 1)

            def ln_scale(i, kind, t, g):
                dve.wait_ge(s_xn, 4 * (2 * i + kind) + t + 1)
                V.tensor_tensor(x_tok[:, t, :], x_tok[:, t, :], g, ALU.mult).then_inc(s_xg, 1)

            def add_and_norm(i):
                dve.wait_ge(s_vmix, 32 * (i + 1))
                for t in range(NT):
                    for n in range(2):
                        K = 8 * i + 2 * t + n
                        dve.wait_ge(op_full, K + 1)
                        xs = x_tok[:, t, n * 512:(n + 1) * 512]
                        last = V.scalar_tensor_tensor(xs, xs, ALPHA, bank[2 + K % 4][:, :], ALU.mult, ALU.add).then_inc(op_out, 1)
                    dve.wait_ge(op_out, 8 * i + 2 * t + 2)
                    ln_stats(i, 0, t)
                    ln_bias(i, 0, t)
                    ln_scale(i, 0, t, vec_mix[:, 0, :])

            def one_hots(w, link=link):
                link(V.tensor_scalar(rwin[:, :, :], rsel[:, :, :], float(-w * P), None, ALU.add))
                for t in range(NT):
                    last = V.tensor_tensor(onehot[t], rwin[:, t, :].unsqueeze(2).to_broadcast([P, NE, P]),
                                           slots_bf[:, :].unsqueeze(1).to_broadcast([P, NE, P]), ALU.is_equal)
                return last

            def table(link=link):
                sums = bank[4][:, 0:2 * NE].rearrange("p (e k) -> p e k", k=2)
                link(V.tensor_copy(route[:, 192:224], bank[4][:, 0:2 * NE]))
                two = route[:, 192:224].rearrange("p (e k) -> p e k", k=2)
                return V.tensor_tensor(idx_i[:, :], two[:, :, 0], two[:, :, 1], ALU.add)

            def router(i):
                off = [14336 + 64]

                def tmp(n):
                    off[0] += n
                    return work[:, off[0] - n:off[0]]
                pr = r_probs
                te = pr.rearrange("p (t e) -> p t e", t=NT)
                gx = pr.rearrange("p (g x) -> p g x", x=GS)
                t1, c1, oh1, oh2, pr2, rk = (tmp(64) for _ in range(6))
                v3 = lambda a: a.rearrange("p (g x) -> p g x", x=GS)
                t3 = lambda a: a.rearrange("p (t e) -> p t e", t=NT)
                g1, g2, mk, gsum, geq, ohg, m1, m2 = (tmp(16) for _ in range(8))
                gm, p1, p2, den = (tmp(4) for _ in range(4))
                over = lambda a, n: a.unsqueeze(2).to_broadcast([P, a.shape[1], n])
                key = key4[:, :].unsqueeze(1).to_broadcast([P, NT * NG, GS])
                key_g = key4[:, :].unsqueeze(1).to_broadcast([P, NT, NG])

                def first_max(src3, mx, oh3, t3_, c3, mk_, n, key_):
                    link(V.tensor_reduce(mx, src3, AX.X, ALU.max))
                    link(V.tensor_tensor(t3_, src3, over(mx, n), ALU.is_equal))
                    link(V.tensor_tensor(c3, t3_, key_, ALU.mult))
                    link(V.tensor_reduce(mk_, c3, AX.X, ALU.max))
                    link(V.tensor_tensor(oh3, c3, over(mk_, n), ALU.is_equal))

                dve.wait_ge(lg_full, i + 1)
                link(V.tensor_tensor(te, bank[6][:, 0:NT * NE].rearrange("p (t e) -> p t e", t=NT),
                                     b_rt[:, :].unsqueeze(1).to_broadcast([P, NT, NE]), ALU.add))
                link(V.tensor_reduce(gm, te, AX.X, ALU.max))
                V.tensor_tensor(te, te, over(gm, NE), ALU.subtract).then_inc(s_lg, 1)
                dve.wait_ge(s_ex, i + 1)
                link(V.tensor_reduce(den, te, AX.X, ALU.add))
                link(V.reciprocal(den, den))
                link(V.tensor_tensor(te, te, over(den, NE), ALU.mult))
                first_max(gx, g1, v3(oh1), v3(t1), v3(c1), mk, GS, key)
                link(V.scalar_tensor_tensor(pr2, oh1, -4.0, pr, ALU.mult, ALU.add))
                first_max(v3(pr2), g2, v3(oh2), v3(t1), v3(c1), mk, GS, key)
                link(V.tensor_tensor(gsum, g1, g2, ALU.add))
                first_max(v3(gsum), gm, v3(ohg), v3(geq), v3(m1), p1, NG, key_g)
                V.tensor_tensor(v3(oh1), v3(oh1), over(ohg, GS), ALU.mult)
                V.tensor_tensor(m1, g1, ohg, ALU.mult)
                link(V.tensor_tensor(v3(oh2), v3(oh2), over(ohg, GS), ALU.mult))
                V.tensor_tensor(m2, g2, ohg, ALU.mult)
                V.tensor_tensor(mask_bf[:, :, :], t3(oh1), t3(oh2), ALU.add).then_inc(s_mask, 1)
                link(V.tensor_tensor(c1, oh1, oh2, ALU.add))
                link(V.tensor_reduce(p1, v3(m1), AX.X, ALU.add))
                link(V.tensor_reduce(p2, v3(m2), AX.X, ALU.add))
                link(V.tensor_tensor(den, p1, p2, ALU.add))
                link(V.reciprocal(den, den))
                V.tensor_tensor(wgt[:, 0, :], p1, den, ALU.mult)
                link(V.tensor_tensor(wgt[:, 1, :], p2, den, ALU.mult))
                dve.wait_ge(rk_full, i + 1)
                link(V.tensor_copy(rk, bank[3][:, 0:64]))
                link(V.tensor_reduce(m1[:, 0:1], bank[3][:, 64:80], AX.X, ALU.max))
                V.tensor_copy(most_i[:, :], m1[:, 0:1]).then_inc(s_most, 1)
                link(V.scalar_tensor_tensor(rsel, t3(rk), 1.0, t3(c1), ALU.add, ALU.mult))
                link(V.tensor_scalar(rsel, rsel, 1.0, None, ALU.subtract))
                one_hots(0).then_inc(s_onehot, 1)
                dve.wait_ge(id_full, i + 1)
                table().then_inc(s_idx, 1)
                link(V.tensor_tensor(t3(t1), t3(rk), e_base[:, :].unsqueeze(1).to_broadcast([P, NT, NE]), ALU.add))
                for w in range(1, WINDOWS):
                    link(V.tensor_scalar(pr2, rk, float(w * P), float((NE - 1) * P), ALU.is_ge, ALU.mult))
                    link(V.tensor_tensor(t1, t1, pr2, ALU.add))
                for k, oh in enumerate((oh1, oh2)):
                    link(V.tensor_tensor(pr2, t1, oh, ALU.mult))
                    link(V.tensor_reduce(p1, t3(pr2), AX.X, ALU.add))
                    link(V.tensor_copy(pos_i[:, 0, k, :], p1))
                    for w in range(1, WINDOWS):
                        link(V.tensor_scalar(p1, p1, float(-NE * P), None, ALU.add))
                        link(V.tensor_scalar(p2, p1, 0.0, float(8 * NE * P), ALU.is_lt, ALU.mult))
                        link(V.tensor_tensor(pos_i[:, w, k, :], p1, p2, ALU.add))

            def experts(i):
                N0 = NE * i

                def hT_copy(par, E):
                    dve.wait_ge(ht_full, E + 1)
                    V.tensor_copy(hT[par], bank[0][:, :]).then_inc(ht_out, 1)

                def hidden(par, E):
                    dve.wait_ge(s_th, E + 1)
                    V.scalar_tensor_tensor(th[par], th[par], 1.0, bank[2 + 2 * par][:, :], ALU.add, ALU.mult).then_inc(s_hg, 1)
                    dve.wait_ge(s_hg, E + 1)
                    dve.wait_ge(u_full, E + 1)
                    V.scalar_tensor_tensor(hh[par], th[par], 0.5, bank[3 + 2 * par][:, :], ALU.mult, ALU.mult).then_inc(s_h, 1)

                hidden(0, N0)
                with dve.Fori(0, NE // 2 - 1) as j:
                    hT_copy(0, 2 * j + N0)
                    hidden(1, 2 * j + (N0 + 1))
                    hT_copy(1, 2 * j + (N0 + 1))
                    hidden(0, 2 * j + (N0 + 2))
                hT_copy(0, N0 + NE - 2)
                hidden(1, N0 + NE - 1)
                hT_copy(1, N0 + NE - 1)

            def window(i, w):
                step, own = ov[i, w][2], ov[i, w][4]

                def link_1(inst):
                    inst.then_inc(own, 1)
                    dve.wait_ge(own, 1)

                def link_2(inst):
                    inst.then_inc(own, 1)
                    dve.wait_ge(own, 2)
                one_hots(w, link_1).then_inc(step, 1)
                dve.wait_ge(step, 2)
                table(link_2).then_inc(step, 1)
                with dve.Fori(0, NE) as e:
                    def before(name):
                        dve.wait_ge(step, e * OV + (at[name] - 1))
                    before("silu")
                    V.scalar_tensor_tensor(th[0], th[0], 1.0, bank[2][:, :], ALU.add, ALU.mult).then_inc(step, 1)
                    before("h")
                    V.scalar_tensor_tensor(hh[0], th[0], 0.5, bank[3][:, :], ALU.mult, ALU.mult).then_inc(step, 1)
                    before("hT_out")
                    V.tensor_copy(hT[0], bank[0][:, :]).then_inc(step, 1)
                dve.wait_ge(step, OV * NE + OV_ROUTE)

            def combine_and_ple(i):
                dve.wait_ge(s_vffn, 48 * (i + 1))

                def combine(t):
                    y = yg[t % 2]
                    dve.wait_ge(s_y1, NT * i + t + 1)
                    link(V.scalar_tensor_tensor(y[:, 0, :], y[:, 1, :], wgt[:, 1, t:t + 1], y[:, 0, :], ALU.mult, ALU.add))
                    V.scalar_tensor_tensor(x_tok[:, t, :], x_tok[:, t, :], ALPHA, y[:, 0, :], ALU.mult, ALU.add).then_inc(s_comb, 1)
                    dve.wait_ge(s_comb, NT * i + t + 1)
                    ln_stats(i, 1, t)
                    ln_bias(i, 1, t)
                    ln_scale(i, 1, t, vec_ffn[:, 0, :])

                def biased(t, n):
                    K = 8 * i + 2 * t + n
                    dve.wait_ge(pg_full, K + 1)
                    wait(dve, s_px, K - 1)
                    V.tensor_tensor(gt[n], bank[2 + K % 4][:, :], b_ple[:, n * 512:(n + 1) * 512], ALU.add).then_inc(s_pg, 1)

                def gated(t, n):
                    K = 8 * i + 2 * t + n
                    dve.wait_ge(s_pt, K + 1)
                    V.scalar_tensor_tensor(gt[n], gt[n], 1.0, bank[6 + n][:, :], ALU.add, ALU.mult).then_inc(s_pp, 1)
                    dve.wait_ge(s_pp, K + 1)
                    xs = x_tok[:, t, n * 512:(n + 1) * 512]
                    return V.scalar_tensor_tensor(xs, gt[n], 0.5, xs, ALU.mult, ALU.add).then_inc(s_px, 1)

                combine(0)
                combine(1)
                for t in range(NT):
                    biased(t, 0)
                    biased(t, 1)
                    gated(t, 0)
                    gated(t, 1)
                    if t + 2 < NT:
                        combine(t + 2)

            def qkv():
                dve.wait_ge(s_rope, 3)
                for t in range(NT):
                    r = raw[t % 2]
                    dve.wait_ge(qkv_out, 3 * t + 3)
                    if t >= 2:
                        dve.wait_ge(tr_full, TR_QKV + 3 * (t - 1))
                    link(V.tensor_tensor(rope_a.rearrange("p (h f) -> p h f", f=32), r.rearrange("p (h f) -> p h f", f=32),
                                         cos_t[:, t, :].unsqueeze(1).to_broadcast([P, 40, 32]), ALU.mult))
                    dve.wait_ge(s_ropeb, t + 1)
                    V.tensor_tensor(rot[t % 2][:, 0:1024], rope_a[:, 0:1024], rope_b[:, 0:1024], ALU.add)
                    kd = rot[t % 2][:, 1024:1536].rearrange("p (k two d) -> p k two d", k=SWA_KV, two=2)
                    for c in range(2):
                        last = V.tensor_tensor(kd[:, :, c, :], rope_a[:, 1024:1280].rearrange("p (k d) -> p k d", d=HD),
                                               rope_b[:, 1024:1280].rearrange("p (k d) -> p k d", d=HD), ALU.add)
                    last.then_inc(s_rot, 1)
                    dve.wait_ge(s_rot, t + 1)

            def swa():
                def softmax_in(u):
                    b, kv = divmod(u, SWA_KV)
                    lo = 0 if b else P
                    s_, m = sc[u % 3], sm[:, u % 4, :]
                    dve.wait_ge(sc_full, u + 1)
                    wait(dve, pt_full, u - 2)
                    for k in range(2):
                        src = bank[2 + 2 * (u % 2) + k][:, :].rearrange("p (h s) -> p h s", h=2)
                        last = V.scalar_tensor_tensor(s_[:, k::2, lo:], src[:, :, lo:], HD ** -0.5,
                                                      band[:, lo:].unsqueeze(1).to_broadcast([P, 2, 2 * P - lo]), ALU.mult, ALU.add)
                    last.then_inc(sc_out, 1)
                    dve.wait_ge(sc_out, u + 1)
                    link(V.tensor_reduce(m[:, 0:4], s_[:, :, lo:], AX.X, ALU.max))
                    link(V.tensor_tensor(m[:, 0:4], m[:, 0:4], sinks[:, GRP * kv:GRP * (kv + 1)], ALU.max))
                    V.tensor_scalar(m[:, 4:8], m[:, 0:4], -1.0, None, ALU.mult)
                    V.tensor_tensor(m[:, 12:16], sinks[:, GRP * kv:GRP * (kv + 1)], m[:, 0:4], ALU.subtract).then_inc(s_nm, 1)

                def normed(u):
                    b, kv = divmod(u, SWA_KV)
                    m = sm[:, u % 4, :]
                    dve.wait_ge(s_pr, u + 1)
                    link(V.tensor_tensor(m[:, 16:20], m[:, 8:12], m[:, 12:16], ALU.add))
                    link(V.reciprocal(m[:, 16:20], m[:, 16:20]))
                    dve.wait_ge(pv_full, u + 1)
                    if kv == 0 and b >= 2:
                        dve.wait_ge(tr_full, TR_SWA + 2 * (b - 1))
                    V.tensor_tensor(y_sw[b % 2][:, kv * 256:(kv + 1) * 256].rearrange("p (h d) -> p h d", h=GRP),
                                         bank[6 + u % 2][:, 0:256].rearrange("p (h d) -> p h d", h=GRP),
                                         m[:, 16:20].unsqueeze(2).to_broadcast([P, GRP, HD]), ALU.mult).then_inc(pv_out, 1)

                softmax_in(0)
                softmax_in(1)
                for u in range(UNITS + 1):
                    if u + 2 < UNITS:
                        softmax_in(u + 2)
                    if u >= 1:
                        normed(u - 1)

            for i in range(DEPTH):
                if i == 1:
                    qkv()
                    swa()
                add_and_norm(i)
                router(i)
                experts(i)
                overflow(dve, i, window)
                combine_and_ple(i)

        @block.gpsimd
        def _(pool):
            G = nc.gpsimd
            n_seq = [0]

            def link(inst):
                inst.then_inc(s_pool, 1)
                n_seq[0] += 1
                pool.wait_ge(s_pool, n_seq[0])

            def select(ap, op, fill, base, pattern, mult):
                return G.affine_select(out=ap, in_=ap, pattern=pattern, compare_op=op, fill=fill, base=base, channel_multiplier=mult)

            link(G.memset(ident[:, :], 0.0))
            select(ident[:, :], ALU.not_equal, 1.0, 0, [[-1, P]], 1).then_inc(s_ident, 1)
            G.memset(w_bd[:, :, :, :], 0.0).then_inc(s_const, 1)
            for f in range(32):
                last = G.memset(band[:, f:f + 1], 10000.0 ** (-f / 32))
            last.then_inc(s_const, 1)
            G.memset(neg_tri[:, :], -1.0)
            G.memset(neg_ones[:, :], -1.0)
            G.memset(stri_bf[:, :], 1.0)
            G.memset(ones_bf[:, :], 1.0)
            G.memset(mhalf[:, :], -0.5)
            for k in range(4):
                G.memset(key4[:, k:k + 1], float(4 - k))
            link(G.iota(slot_i, pattern=[[1, P]], base=0, channel_multiplier=0))
            link(G.tensor_copy(slots_bf[:, :], slot_i))
            link(G.iota(slot_i[:, 0:NE], pattern=[[P, NE]], base=0, channel_multiplier=0))
            link(G.tensor_copy(e_base[:, :], slot_i[:, 0:NE]))
            link(G.iota(slot_i[:, 0:NT], pattern=[[0, NT]], base=0, channel_multiplier=1))
            link(G.tensor_copy(tok_id[:, :, 0], slot_i[:, 0:NT]))
            link(G.iota(slot_i[:, 0:NT], pattern=[[P, NT]], base=0, channel_multiplier=0))
            link(G.tensor_copy(tok_id[:, :, 1], slot_i[:, 0:NT]))
            select(neg_tri[:, :], ALU.is_ge, 0.0, 0, [[-1, P]], 1)
            select(stri_bf[:, :], ALU.is_gt, 0.0, 0, [[1, P]], -1).then_inc(s_const, 1)
            pool.wait_ge(s_rope, 2)
            link(G.memset(band[:, :], 0.0))
            link(select(band[:, :], ALU.is_ge, NEG, P, [[-1, 2 * P]], 1))
            link(select(band[:, :], ALU.is_gt, NEG, 0, [[1, 2 * P]], -1))
            G.tensor_scalar(sin_t[:, 0, :, :], sin_t[:, 1, :, :], -1.0, None, ALU.mult).then_inc(s_rope, 1)

            def mask(t, done):
                for kt in range(NT):
                    last = select(t[:, SEG[kt]:SEG[kt] + P], ALU.is_gt, 0.0, 0, [[1, P]], -1)
                last.then_inc(done, 1)

            def softplus_mask(h):
                pool.wait_ge(s_sp, h + 1)
                mask(tb[h % 2], s_spm)

            softplus_mask(0)
            for h in range(SBH):
                if h + 1 < SBH:
                    softplus_mask(h + 1)
                pool.wait_ge(s_w, h + 1)
                mask(zb[h % 3], s_wm)

            def ln_parts(i, kind, t, b):
                K = 4 * (2 * i + kind) + t + 1
                pool.wait_ge(s_ve, K)
                G.tensor_tensor(lnp[:, t, 1:2], lnp[:, t, 0:1], mhalf[:, :], ALU.pow).then_inc(s_rstd, 1)
                pool.wait_ge(s_xg, K)
                G.tensor_tensor(x_tok[:, t, :], x_tok[:, t, :], b, ALU.add).then_inc(s_xln, 1)

            def gather(dst, rows, index, done, **bound):
                G.indirect_dma_start(dst, None, rows, bass.IndirectOffsetOnAxis(ap=index, axis=0), **bound).then_inc(done, 16)

            def experts(i):
                N0 = NE * i
                pool.wait_ge(s_idx, i + 1)
                pool.wait_ge(s_xd, 64 * (i + 1))
                for e in range(NE):
                    if e >= 2:
                        pool.wait_ge(xb_full, N0 + e - 1)
                    gather(xe[e % 2], x_dram[i], idx_i[:, e:e + 1], xe_full[e % 2])

            def window(i, w):
                _, loaded, step = ov[i, w][:3]
                for e in range(NE):
                    pool.wait_ge(step, OV * e + OV_ROUTE)
                    gather(xe[0], x_dram[i], idx_i[:, e:e + 1], ov[i, w][6])
                pool.wait_ge(step, OV * NE + OV_ROUTE)
                pool.wait_ge(ov[i, w][3], 16 * NE)

            def combine(i, most):
                for s in y_wr:
                    pool.wait_ge(s, 16 * (NE // 2) * (i + 1))
                def rows(t):
                    wait(pool, s_comb, NT * i + t - 1 if t >= 2 else 0)
                    for w in range(1, WINDOWS):
                        with pool.If(most > w * P):
                            for k in range(2):
                                gather(yg[t % 2][:, k, :], y_dram[i][w], pos_i[:, w, k, t:t + 1], ov[i, w][5],
                                       bounds_check=NE * P - 1, oob_is_err=False)
                            pool.wait_ge(ov[i, w][5], 32 * (t + 1))
                    for k in range(2):
                        gather(yg[t % 2][:, k, :], y_dram[i][0], pos_i[:, 0, k, t:t + 1], s_yg[t % 2],
                               bounds_check=NE * P - 1, oob_is_err=False)
                rows(0)
                rows(1)
                for t in range(NT):
                    ln_parts(i, 1, t, vec_ffn[:, 1, :])
                    if t + 2 < NT:
                        rows(t + 2)

            def rope():
                for t in range(NT):
                    r = raw[t % 2].rearrange("p (h two f) -> p h two f", two=2, f=32)
                    o = rope_b.rearrange("p (h two f) -> p h two f", two=2, f=32)
                    pool.wait_ge(qkv_out, 3 * t + 3)
                    wait(pool, s_rot, t)
                    for k in range(2):
                        last = G.tensor_tensor(o[:, :, k, :], r[:, :, 1 - k, :],
                                               sin_t[:, k, t, :].unsqueeze(1).to_broadcast([P, 20, 32]), ALU.mult)
                    last.then_inc(s_ropeb, 1)

            for i in range(DEPTH):
                if i == 1:
                    rope()
                for t in range(NT):
                    ln_parts(i, 0, t, vec_mix[:, 1, :])
                experts(i)
                combine(i, overflow(pool, i, window))


_INS = ["x", "p", "positions", "w_in_ab", "w_out_ab", "conv_w", "conv_b", "lru_w_r", "lru_b_r", "lru_w_i",
        "lru_b_i", "lru_lambda", "w_qkv_c", "w_out_c", "sinks_c", "ln_mix_g", "ln_mix_b", "ln_ffn_g",
        "ln_ffn_b", "w_router", "b_router", "exp_w_gate", "exp_w_up", "exp_w_down", "ple_w_proj",
        "ple_w_gate", "ple_b_gate"]


def kernel(**inputs):
    import numpy as _np
    import concourse.bacc as _bacc
    from concourse import mybir as _mybir
    from concourse.bass_utils import run_bass_kernel_spmd as _run

    nc = _bacc.Bacc("TRN2", target_bir_lowering=False, num_devices=1)
    arrays, args = {}, []
    for name in _INS:
        a = _np.ascontiguousarray(inputs[name])
        arrays[f"in_{name}_dram"] = a
        args.append(nc.dram_tensor(f"in_{name}_dram", a.shape, _mybir.dt.from_np(a.dtype), kind="ExternalInput").ap())
    args.append(nc.dram_tensor("out_0_dram", (1, S, D), _mybir.dt.float32, kind="ExternalOutput").ap())
    trunk(nc, *args)
    r = _run(nc, [arrays], core_ids=[0])
    return r.results[0]["out_0_dram"]
```

```python
import concourse.bass as bass
from concourse import mybir
from contextlib import ExitStack

F32 = mybir.dt.float32
F32R = mybir.dt.float32r
BF16 = mybir.dt.bfloat16
I32 = mybir.dt.int32
ALU = mybir.AluOpType
ACT = mybir.ActivationFunctionType
AX = mybir.AxisListType

P = 128
D = 1024
S = 512
DEPTH = 2
NT = S // P
DC = D // P
HD = 64
SBH = 8
SBW = SBH * HD
LRU = 512
LC = LRU // P
SWA_H, SWA_KV = 16, 4
GRP = SWA_H // SWA_KV
NE, NG, GS = 16, 4, 4
DFF = 512
FC = DFF // P
PLE = 256
ALPHA = (2 * DEPTH) ** 0.25
EPS = 1e-5
NEG = -1e30
SLOTS = 6
SLOT_W = DC * 512
WINDOWS = S // P
L_OUT = (5, 61)
L_MOE = (7, 63)
L_PLE = (55, 111)
L_QKV = 58
SEG = {0: 0, 1: 512, 3: 896, 2: 1024}
SEGW = 1280
TR_QKV = 35
UNITS = SWA_KV * NT
TR_SWA = TR_QKV + 3 * NT
TR_PLE = (TR_QKV - 4 * NT, TR_SWA + 4 * NT + 2)
PI = 3.14159265
TWO_PI = 6.283185307179586
TURN = (6.28125, 2029 / 2 ** 20, TWO_PI - 6.28125 - 2029 / 2 ** 20)


def trunk(nc, x, p, positions, w_in_ab, w_out_ab, conv_w, conv_b, lru_w_r, lru_b_r, lru_w_i,
          lru_b_i, lru_lambda, w_qkv_c, w_out_c, sinks_c, ln_mix_g, ln_mix_b, ln_ffn_g, ln_ffn_b,
          w_router, b_router, exp_w_gate, exp_w_up, exp_w_down, ple_w_proj, ple_w_gate,
          ple_b_gate, out):
    with ExitStack() as ctx:
        def sb(name, shape, dt=F32):
            return ctx.enter_context(nc.sbuf_tensor(name, shape, dt))

        def sem(name):
            return ctx.enter_context(nc.semaphore(name))

        ring = sb("ring", [P, SLOTS * SLOT_W])
        ring_at = nc.sbuf_base - SLOTS * SLOT_W * 4
        x_tok = sb("x_tok", [P, NT, D])
        xT = sb("xT", [P, DC, S])
        rounded = [nc.alloc_sbuf_tensor_at(f"rounded{k}", [P, DC, 512], F32R, offset=ring_at + k * SLOT_W * 4) for k in range(SLOTS)]
        x_high = nc.alloc_sbuf_tensor_at("x_high", [P, DC, S], F32R, offset=nc.sbuf_base - DC * S * 4)
        vec_mix = sb("vec_mix", [P, 2, D])
        w_bd = sb("w_bd", [P, 2, LC, P])
        work = sb("work", [P, 15360])
        x_low_ple = nc.alloc_sbuf_tensor_at("x_low_ple", [P, DC, S], F32R, offset=nc.sbuf_base - (15360 - 10240) * 4)
        ident = sb("ident", [P, P])
        neg_tri = sb("neg_tri", [P, P])
        neg_ones = sb("neg_ones", [P, P])
        band = sb("band", [P, 2 * P])
        cos_t = sb("cos_t", [P, NT, 32])
        sin_t = sb("sin_t", [P, 2, NT, 32])
        w_rt = sb("w_rt", [P, DC, NE])
        b_rt = sb("b_rt", [P, NE])
        sinks = sb("sinks", [P, SWA_H])
        lru_p = sb("lru_p", [P, 8, LC])
        conv_p = sb("conv_p", [P, 4, LC])
        slots_bf = sb("slots_bf", [P, P], BF16)
        stri_bf = sb("stri_bf", [P, P], BF16)
        ones_bf = sb("ones_bf", [P, P], BF16)
        tok_id = sb("tok_id", [P, NT, 2], BF16)
        key4 = sb("key4", [P, 4])
        e_base = sb("e_base", [P, NE])
        mhalf = sb("mhalf", [P, 1])
        route = sb("route", [P, 256])
        mask_bf = sb("mask_bf", [P, NT, NE], BF16)
        idx_i = sb("idx_i", [P, NE], I32)
        pos_i = sb("pos_i", [P, WINDOWS, 2, NT], I32)
        most_i = sb("most_i", [P, 1], I32)
        st = sb("st", [P, NT, 2, 6])
        mv = sb("mv", [P, NT, 2])
        lnp = sb("lnp", [P, NT, 4])
        sm = sb("sm", [P, 4, 24])
        bank = [ctx.enter_context(nc.psum_tensor(f"bank{i}", [P, 512], F32)) for i in range(8)]
        x_dram = [nc.dram_tensor(f"x_rows{i}", [S, D], F32).ap() for i in range(DEPTH)]
        y_dram = [[nc.dram_tensor(f"y_rows{i}_{w}", [NE * P, D], F32).ap() for w in range(WINDOWS)] for i in range(DEPTH)]

        def wk(at, n):
            return work[:, at:at + n]

        def w_raw(k):
            return slot(k % 3).rearrange("p (c n) -> p c n", c=DC)

        def split_at(n):
            return [n + 4] if n < 12 else {12: [16, 17], 13: [18, 19]}.get(n, [])

        def ple_raw(i, n):
            return slot(L_PLE[i] + n).rearrange("p (c n) -> p c n", c=DC)

        def ple_parts(i, n):
            return rounded[((0, 5), (0, 1))[i][n]], rounded[(L_PLE[i] + n) % SLOTS]

        def ring_times(n):
            return n // SLOTS + (n % SLOTS == 5)

        def proj_bank(n):
            return 2 + n % 4 if n < 16 else (5, 6, 7, 1)[n - 16]

        def slot(n):
            s = n % SLOTS
            return ring[:, s * SLOT_W:(s + 1) * SLOT_W]

        qT = wk(0, 2048).rearrange("p (c s) -> p c s", c=4)
        kT = wk(2048, 2048).rearrange("p (c s) -> p c s", c=4)
        v0 = wk(4096, 2048).rearrange("p (t n) -> p t n", t=NT)
        gr = wk(6144, 2048).rearrange("p (c s) -> p c s", c=LC)
        xr = wk(8192, 2048).rearrange("p (c s) -> p c s", c=LC)
        xc = wk(10240, 2048).rearrange("p (c s) -> p c s", c=LC)
        gi = wk(12288, 2048).rearrange("p (c s) -> p c s", c=LC)
        r_t = wk(14336, 512)
        r_d = wk(14848, 512)
        rows = work[0:36, 0:P]
        pos_row = work[32:36, P:2 * P].bitcast(I32)
        slot_i = wk(14336, P).bitcast(I32)
        turns_i = wk(14848, P).bitcast(I32).rearrange("p (t f) -> p t f", t=NT)
        zb = [wk(8192 + SEGW * i, SEGW) for i in range(3)]
        tb = [wk(12032 + SEGW * i, SEGW) for i in range(2)]
        raw = [wk(1280 * i, 1280) for i in range(2)]
        rope_a, rope_b = wk(2560, 1280), wk(3840, 1280)
        rot = [wk(5120 + 1536 * i, 1536) for i in range(2)]
        qT1 = wk(8192, 4096).rearrange("p (c s) -> p c s", c=8)
        kT1 = wk(12288, 2048).rearrange("p (c s) -> p c s", c=4)
        v1 = wk(14336, 1024).rearrange("p (t n) -> p t n", t=NT)
        sc = [wk(at, 1024).rearrange("p (h s) -> p h s", h=GRP) for at in (0, 1024, 6144)]
        pT1 = [wk(2048 + 1024 * i, 1024).rearrange("p (j n) -> p j n", j=2) for i in range(2)]
        y_sw = [wk(4096 + 1024 * i, 1024) for i in range(2)]
        vec_ffn = wk(0, 2048).rearrange("p (k n) -> p k n", k=2)
        b_ple = wk(2048, 1024)
        p_tok = wk(3072, 1024).rearrange("p (t n) -> p t n", t=NT)
        pT = wk(4096, 1024).rearrange("p (c s) -> p c s", c=2)
        xe = [wk(5120 + 1024 * i, 1024) for i in range(2)]
        xeT = [wk(7168 + 1024 * i, 1024).rearrange("p (c s) -> p c s", c=DC) for i in range(2)]
        hh = [wk(9216 + 512 * i, 512) for i in range(2)]
        hT = [wk(10240 + 512 * i, 512) for i in range(2)]
        th = [wk(11264 + 512 * i, 512) for i in range(2)]
        yy = [wk(12288 + 1024 * i, 1024) for i in range(2)]
        onehot = [wk(10240 + 1024 * t, 1024).bitcast(BF16).rearrange("p (s e) -> p s e", e=NE) for t in range(NT)]
        places = w_bd[:, :, :, :].rearrange("p k c o -> p (k c o)").bitcast(BF16).rearrange("p (s e) -> p s e", e=NE)
        yg = [wk(5120 + 2048 * i, 2048).rearrange("p (k n) -> p k n", k=2) for i in range(2)]
        gt = [wk(9216 + 512 * i, 512) for i in range(2)]
        r_probs = wk(14336, 64)
        rsel = route[:, 0:64].rearrange("p (t e) -> p t e", t=NT)
        rwin = route[:, 64:96].bitcast(BF16).rearrange("p (t e) -> p t e", t=NT)
        wgt = route[:, 128:136].rearrange("p (k t) -> p k t", k=2)

        s_x = [sem(f"x_loaded{t}") for t in range(NT)]
        s_w0 = sem("first_weights_loaded")
        in_full = [sem(f"in_weights_loaded{k}") for k in range(5)]
        s_whi = sem("weights_high_ready")
        s_wlo = sem("weights_low_ready")
        s_xlo = sem("x_low_ready")
        s_small = sem("small_loaded")
        s_bd = sem("gates_loaded")
        s_vmix = sem("ln_mix_loaded")
        s_vffn = sem("ln_ffn_loaded")
        s_p = sem("p_loaded")
        s_posn = sem("positions_loaded")
        s_posf = sem("positions_cast")
        ring_full = [sem(f"ring_full{i}") for i in range(SLOTS)]
        s_ident = sem("ident_made")
        s_pool = sem("pool_step")
        s_const = sem("consts_made")
        s_dve = sem("dve_step")
        s_act = sem("act_step")
        tr_full = sem("transposed")
        tr_out = sem("transposed_copied")
        proj_full = sem("proj_summed")
        proj_out = sem("proj_copied")
        s_lrup = sem("lru_params_ready")
        s_conv = sem("conv_ready")
        gate_full = sem("lru_gates_summed")
        gate_out = sem("lru_gates_read")
        s_T = sem("lru_tanh_ready")
        s_u2 = sem("lru_u2_ready")
        s_sq = sem("lru_root_ready")
        s_lru = sem("lru_ready")
        z_full = sem("z_summed")
        z_out = sem("z_copied")
        s_neg = sem("neg_abs_ready")
        s_ln1p = sem("log1p_ready")
        s_sp = sem("softplus_ready")
        s_spm = sem("softplus_masked")
        c_full = sem("after_summed")
        s_arg = sem("arg_ready")
        s_w = sem("w_ready")
        s_wm = sem("w_masked")
        y_full = sem("y_summed")
        y_out = sem("y_copied")
        op_full = sem("out_proj_summed")
        op_out = sem("out_proj_added")
        s_ve = sem("ln_var_ready")
        s_rstd = sem("ln_rstd_ready")
        s_xc = sem("ln_centred")
        s_xln = sem("ln_ready")
        s_xd = sem("x_rows_written")
        lg_full = sem("logits_summed")
        s_lg = sem("logits_shifted")
        s_ex = sem("router_exp_ready")
        s_mask = sem("mask_ready")
        rk_full = sem("ranks_summed")
        s_onehot = sem("onehot_ready")
        id_full = sem("table_summed")
        s_idx = sem("table_ready")
        s_most = sem("most_ready")
        xe_full = [sem(f"xe_gathered{i}") for i in range(2)]
        xa_full = sem("xe_low_transposed")
        xa_out = sem("xe_low_copied")
        xb_full = sem("xe_high_transposed")
        xb_out = sem("xe_high_copied")
        g_full = sem("gate_summed")
        u_full = sem("up_summed")
        s_th = sem("tanh_ready")
        s_hg = sem("silu_ready")
        s_h = sem("hidden_ready")
        ht_full = sem("hidden_transposed")
        ht_out = sem("hidden_copied")
        ye_full = sem("expert_out_summed")
        ye_out = sem("expert_out_copied")
        y_wr = [sem(f"y_rows_written{i}") for i in range(2)]
        s_yg = [sem(f"y_rows_gathered{i}") for i in range(2)]
        s_xa = sem("x_times_alpha")
        s_comb = sem("combined")
        pg_full = sem("ple_gate_summed")
        s_pg = sem("ple_gate_biased")
        s_pt = sem("ple_tanh_ready")
        s_pp = sem("ple_proj_read")
        s_px = sem("ple_added")
        s_ang = sem("angles_ready")
        s_rope = sem("rope_tables_ready")
        qkv_full = sem("qkv_summed")
        qkv_out = sem("qkv_copied")
        s_ropeb = sem("rope_swapped")
        s_rot = sem("rotated")
        sc_full = sem("scores_summed")
        sc_out = sem("scores_masked")
        s_nm = sem("max_ready")
        s_pr = sem("probs_ready")
        pt_full = sem("probs_transposed")
        pt_prev = sem("probs_prev_copied")
        pt_cur = sem("probs_cur_copied")
        pv_full = sem("pv_summed")
        pv_out = sem("pv_normed")
        s_out = sem("out_written")
        ov = {(i, w): [sem(f"ov_{n}_{i}_{w}") for n in ("enter", "loaded", "step", "written", "dve", "y_gathered", "x_gathered")]
              for i in range(DEPTH) for w in range(1, WINDOWS)}

        block = ctx.enter_context(nc.Block())

        def wait(eng, s, v):
            if not (isinstance(v, int) and v <= 0):
                eng.wait_ge(s, v)

        def overflow(eng, i, body, stored=()):
            eng.wait_ge(s_most, i + 1)
            most = eng.value_load(most_i[0:1, 0:1], min_val=0, max_val=S)
            for w in range(1, WINDOWS):
                with eng.If(most > w * P):
                    enter = ov[i, w][0]
                    for s in stored:
                        eng.wait_ge(s, 16 * (NE // 2) * (i + 1))
                    eng.drain().then_inc(enter, 1)
                    eng.wait_ge(enter, 5)
                    body(i, w)
            return most

        OV_ROUTE = 3
        OV = 10
        OV_NAMES = ("xeT", "xeT_out", "gu", "tanh", "silu", "h", "hT", "hT_out", "y", "y_out")
        at = {n: OV_ROUTE + k + 1 for k, n in enumerate(OV_NAMES)}

        @block.sync
        def _(sp):
            for t in range(NT):
                sp.dma_start(x_tok[:, t, :], x[0, t * P:(t + 1) * P, :]).then_inc(s_x[t], 16)

            def last_use(n):
                for i in range(DEPTH):
                    if L_OUT[i] <= n < L_OUT[i] + 2:
                        return op_full, 8 * i + 7 + n - L_OUT[i]
                    if L_MOE[i] <= n < L_MOE[i] + 3 * NE:
                        e, k = divmod(n - L_MOE[i], 3)
                        return (g_full, u_full, ye_full)[k], (NE * i + e + 1) * (2 if k == 2 else 1)
                    if L_PLE[i] <= n < L_PLE[i] + 3:
                        return pg_full, 8 * i + min(7 + n - L_PLE[i], 8)
                if L_QKV <= n < L_QKV + 3:
                    return qkv_full, 3 * (NT - 1) + n - L_QKV + 1

            def load(n, src, j=0, e_dst=None):
                if n - SLOTS < L_OUT[0]:
                    sp.wait_ge(proj_full, (16, 20, 12, 20, 16, 20)[n % SLOTS])
                else:
                    s, v = last_use(n - SLOTS)
                    if not isinstance(j, int):
                        v = (4 if s is ye_full else 2) * j + v
                    sp.wait_ge(s, v)
                dst = slot(n)[:, 0:e_dst] if e_dst else slot(n)
                sp.dma_start(dst.rearrange("p (c n) -> p c n", c=src.shape[1]), src)\
                  .then_inc(ring_full[n % SLOTS], 16)

            def cols(w, a):
                return w[:, a:a + 512].rearrange("(p c) n -> p c n", c=DC)

            def out_cols(w, a):
                return w[:, a:a + 512].rearrange("(c p) n -> p c n", c=DC)

            def experts(i):
                def expert_src(e):
                    sel = (lambda w: w[i, e]) if isinstance(e, int) else \
                          (lambda w: w[i, bass.ds(e, 1)].rearrange("o k n -> (o k) n"))
                    return (sel(exp_w_gate).rearrange("(p c) n -> p c n", c=DC),
                            sel(exp_w_up).rearrange("(p c) n -> p c n", c=DC),
                            sel(exp_w_down).rearrange("(p c) n -> p c n", c=FC))
                return expert_src

            def moe(i):
                src = experts(i)
                for e in range(2):
                    for k, s in enumerate(src(e)):
                        load(L_MOE[i] + 3 * e + k, s)
                with sp.Fori(0, NE // 2 - 1) as j:
                    for b in range(2, 4):
                        for k, s in enumerate(src(2 * j + b)):
                            load(L_MOE[i] + 3 * b + k, s, j)

                def window(i, w):
                    _, loaded, step = ov[i, w][:3]
                    own = L_PLE[i] + 3
                    for k in range(3):
                        sp.dma_start(slot(own + k), src(0)[k].rearrange("p c n -> p (c n)")).then_inc(loaded, 16)
                    with sp.Fori(1, NE) as e:
                        sp.wait_ge(step, OV * e + OV_ROUTE)
                        for k, s in enumerate(src(e)):
                            sp.dma_start(slot(own + k), s.rearrange("p c n -> p (c n)")).then_inc(loaded, 16)
                    sp.wait_ge(step, OV * NE + OV_ROUTE)
                return window

            for j in range(4):
                w = w_in_ab[0][:, 1536 + j * P:1536 + (j + 1) * P].rearrange("(p c) n -> p c n", c=DC)
                sp.dma_start(w_raw(0)[:, :, j * P:(j + 1) * P], w).then_inc(s_w0 if j < 3 else in_full[0], 16)
            sp.dma_start(vec_mix[:, 0, :], ln_mix_g[0].partition_broadcast(P)).then_inc(s_vmix, 16)
            sp.dma_start(vec_mix[:, 1, :], ln_mix_b[0].partition_broadcast(P)).then_inc(s_vmix, 16)
            sp.wait_ge(s_const, 1)
            for k, w in enumerate((lru_w_r, lru_w_i)):
                for h in range(2):
                    sp.dma_start(w_bd[h * HD:(h + 1) * HD, k, :, h * HD:(h + 1) * HD],
                                  w[0].rearrange("(c h) i o -> h i c o", h=2)[h]).then_inc(s_bd, 16)
            sp.dma_start(w_rt[:, :, :], w_router.rearrange("(p c) e -> p c e", c=DC)).then_inc(s_bd, 16)
            sp.dma_start(b_rt[:, :], b_router.partition_broadcast(P)).then_inc(s_bd, 16)
            sp.dma_start(sinks[:, :], sinks_c[0].partition_broadcast(P)).then_inc(s_bd, 16)
            for k, a in enumerate((2048, 0, 512, 1024), start=1):
                if k >= 3:
                    sp.wait_ge(proj_full, 4 * (k - 2))
                sp.dma_start(w_raw(k), cols(w_in_ab[0], a)).then_inc(in_full[k], 16)
            for i in range(DEPTH):
                if i == 1:
                    for s in s_yg:
                        sp.wait_ge(s, 32 * 2)
                    for k in range(3):
                        if k == 1:
                            sp.wait_ge(pg_full, 8)
                        load(L_QKV + k, cols(w_qkv_c[0], 512 * k))
                for k in range(2):
                    load(L_OUT[i] + k, out_cols((w_out_ab, w_out_c)[i][0], 512 * k))
                window = moe(i)
                for k in range(2):
                    load(L_PLE[i] + k, cols(ple_w_gate[i], 512 * k))
                load(L_PLE[i] + 2, ple_w_proj[i].rearrange("(c p) n -> p c n", c=2), e_dst=2048)
                overflow(sp, i, window)

        @block.tensor
        def _(pe):
            mm, tr = nc.tensor.matmul, nc.tensor.transpose
            n_tr = [0]

            def weights(n, j=0):
                times = ring_times(n)
                pe.wait_ge(ring_full[n % SLOTS], 16 * (times + j) if isinstance(j, int) else 16 * j + 16 * times)
                return slot(n).rearrange("p (c n) -> p c n", n=512)

            def turn4(src):
                n = n_tr[0]
                wait(pe, tr_out, n - 1)
                wait(pe, s_xlo, min(n - 1, 2 * NT))
                for k in range(4):
                    last = tr(bank[n % 2][:, k * P:(k + 1) * P], src(k), ident[:, :])
                last.then_inc(tr_full, 1)
                n_tr[0] += 1

            def turn_x(t):
                for a in range(2):
                    turn4(lambda k: x_tok[:, t, 4 * a + k::DC])

            def xT_ready():
                pe.wait_ge(tr_out, n_tr[0])

            pe.wait_ge(s_ident, 1)
            for t in range(NT):
                pe.wait_ge(s_x[t], 16)
                turn_x(t)
            pe.wait_ge(s_small, 16 * 5)
            pe.wait_ge(s_posf, 1)
            xT_ready()
            pe.wait_ge(s_xlo, 2 * NT)
            tr(bank[0][:, 0:36], rows, ident[0:36, 0:36]).then_inc(tr_full, 1)
            n_tr[0] += 1

            def z_scores(h):
                r, c = HD * (h % 2), h // 2
                wait(pe, z_out, h)
                for kt in (0, 1, 3, 2):
                    o = SEG[kt]
                    b, o = bank[2 + o // 512], o % 512
                    last = mm(b[:, o:o + S - kt * P], kT[r:r + HD, c, kt * P:(kt + 1) * P], qT[r:r + HD, c, kt * P:S],
                              start=True, stop=True)
                last.then_inc(z_full, 1)

            for n in range(20):
                kind, j = n // 4, n % 4
                if n == 16:
                    pe.wait_ge(proj_out, 16)
                    pe.wait_ge(gate_out, 2 * LC)
                    z_scores(0)
                if n == 19:
                    z_scores(1)
                pe.wait_ge(s_wlo, n + 1 if kind < 4 else 20)
                o = bank[proj_bank(n)]
                if n < 16:
                    wait(pe, proj_out, n - 3)
                hi, lo, cols = rounded[3 + kind % 2], rounded[kind % 3], slice(j * P, (j + 1) * P)
                xh, xl = x_high, rounded[5]
                for c in range(DC):
                    for k, (w, x_) in enumerate(((hi, xh), (hi, xl), (lo, xh))):
                        at_ = dict(start=c == 0 and k == 0, stop=c == DC - 1 and k == 2)
                        if kind < 4:
                            last = mm(o[:, :], w[:, c, cols], x_[:, c, :], **at_)
                        else:
                            last = mm(o[:, :], x_[:, c, cols], w[:, c, :], **at_)
                last.then_inc(proj_full, 1)
                if n in (7, 9, 11, 13):
                    c = (n - 7) // 2
                    if c == 0:
                        pe.wait_ge(s_bd, 16 * 7)
                        pe.wait_ge(s_const, 3)
                    pe.wait_ge(s_conv, c + 1)
                    for k in range(2):
                        wait(pe, gate_out, 2 * c - 1 + k)
                        mm(bank[6 + k][:, :], w_bd[:, k, c, :], xc[:, c, :], start=True, stop=True).then_inc(gate_full, 1)

            def after_sums(h):
                pe.wait_ge(s_spm, h + 1)
                wait(pe, s_arg, h)
                t = tb[h % 2]
                for kt in (0, 1, 3, 2):
                    b, o = bank[5 + SEG[kt] // 512], SEG[kt] % 512
                    for k2 in range(kt, NT):
                        width = S - k2 * P
                        last = mm(b[:, o + (k2 - kt) * P:o + (k2 - kt) * P + width],
                                  (neg_tri if k2 == kt else neg_ones)[:, :], t[:, SEG[k2]:SEG[k2] + width],
                                  start=k2 == kt, stop=k2 == NT - 1)
                last.then_inc(c_full, 1)

            def weigh(h):
                pe.wait_ge(s_wm, h + 1)
                wait(pe, y_out, h - 1)
                pair = 2 * (h // 2) * HD
                for kt in range(NT):
                    last = mm(bank[h % 2][:, kt * P:S], v0[:, kt, pair:pair + 2 * HD], zb[h % 3][:, SEG[kt]:SEG[kt] + S - kt * P],
                              start=kt == 0, stop=kt == NT - 1)
                last.then_inc(y_full, 1)

            def lru_part(K):
                t, n = divmod(K, 2)
                w = weights(L_OUT[0] + n)
                for c in range(LC):
                    mm(bank[2 + K][:, :], gr[:, c, t * P:(t + 1) * P], w[:, LC + c, :], start=c == 0, stop=False)

            pe.wait_ge(proj_out, 20)
            for h in range(SBH + 1):
                if 2 <= h + 1 < SBH:
                    z_scores(h + 1)
                if h == SBH - 1:
                    pe.wait_ge(z_out, SBH)
                    for K in range(2):
                        lru_part(K)
                if h < SBH:
                    after_sums(h)
                if h >= 1:
                    if h == SBH:
                        lru_part(2)
                    weigh(h - 1)
            pe.wait_ge(y_out, SBH)

            def out_proj(i, t):
                for n in range(2):
                    K = 8 * i + 2 * t + n
                    w = weights(L_OUT[i] + n)
                    wait(pe, op_out, K - 3)
                    begun = i == 0 and K < 3
                    chunks = (list(range(DC)) if i == 1 else list(range(LC)) if begun else list(range(LC, DC)) + list(range(LC)))
                    for c in chunks:
                        src = gr[:, c - LC, :] if i == 0 and c >= LC else xT[:, c, :]
                        last = mm(bank[2 + K % 4][:, :], src[:, t * P:(t + 1) * P], w[:, c, :],
                                  start=c == chunks[0] and not begun, stop=c == chunks[-1])
                    last.then_inc(op_full, 1)

            def turn_normed(i, kind, t):
                pe.wait_ge(s_xln, 4 * (2 * i + kind) + t + 1)
                if kind == 1:
                    pe.wait_ge(s_xlo, 2 * NT * (i + 1) + 2 * t)
                turn_x(t)

            def logits(i, t):
                for c in range(DC):
                    last = mm(bank[6][:, t * NE:(t + 1) * NE], xT[:, c, t * P:(t + 1) * P], w_rt[:, c, :],
                              start=c == 0, stop=c == DC - 1)
                if t == NT - 1:
                    last.then_inc(lg_full, 1)

            def out_and_turn(i):
                for t in range(NT + 2):
                    if 2 * i <= t < NT:
                        out_proj(i, t)
                    if t >= 2:
                        xT_ready()
                        logits(i, t - 2)
                    if 1 <= t <= NT:
                        turn_normed(i, 0, t - 1)

            def table_sums(done, ready, value):
                pe.wait_ge(ready, value)
                for e in range(NE):
                    for t in range(NT):
                        last = mm(bank[4][:, 2 * e:2 * e + 2], onehot[t][:, :, e], tok_id[:, t, :], start=t == 0, stop=t == NT - 1)
                last.then_inc(done, 1)

            def router(i):
                pe.wait_ge(s_p, 16 * (i + 1))
                for b in range(2):
                    turn4(lambda k: p_tok[:, 2 * b + k % 2, (k // 2) * P:(k // 2 + 1) * P])
                pe.wait_ge(s_mask, i + 1)
                pe.wait_ge(tr_out, n_tr[0])
                for t in range(NT):
                    for t2 in range(t + 1):
                        mm(bank[7][:, t * NE:(t + 1) * NE], (stri_bf if t2 == t else ones_bf)[:, :], mask_bf[:, t2, :],
                           start=t2 == 0, stop=t2 == t)
                for t in range(NT):
                    last = mm(bank[7][:, NT * NE:(NT + 1) * NE], ones_bf[:, :], mask_bf[:, t, :], start=t == 0, stop=t == NT - 1)
                last.then_inc(rk_full, 1)
                table_sums(id_full, s_onehot, i + 1)

            def experts(i):
                N0 = NE * i
                L = L_MOE[i]

                def turn_xe(half, par, E):
                    b = bank[1 - half]
                    for k in range(4):
                        last = tr(b[:, k * P:(k + 1) * P], xe[par][:, 4 * half + k::DC], ident[:, :])
                    last.then_inc((xa_full, xb_full)[half], 1)

                def gate_up(par, E, n, j, first):
                    pe.wait_ge(xa_out, E + 1)
                    pe.wait_ge(xb_out, E + 1)
                    wait(pe, s_h, E - 1)
                    for k in range(2):
                        w = weights(n + k, j)
                        for c in range(DC):
                            last = mm(bank[2 + 2 * par + k][:, :], xeT[par][:, c, :], w[:, c, :], start=c == 0, stop=c == DC - 1)
                        last.then_inc((g_full, u_full)[k], 1)
                        if k == 0 and not first:
                            turn_hidden(1 - par, E - 1)

                def turn_hidden(par, E):
                    pe.wait_ge(s_h, E + 1)
                    for k in range(FC):
                        last = tr(bank[0][:, k * P:(k + 1) * P], hh[par][:, k::FC], ident[:, :])
                    last.then_inc(ht_full, 1)

                def down(par, E, n, j, half):
                    if half == 0:
                        pe.wait_ge(ht_out, E + 1)
                        weights(n, j)
                    w = slot(n).rearrange("p (c n) -> p c n", n=D)
                    wait(pe, ye_out, 2 * E - 1 + half)
                    for c in range(FC):
                        last = mm(bank[6 + half][:, :], hT[par][:, c * P:(c + 1) * P], w[:, c, half * 512:(half + 1) * 512],
                                  start=c == 0, stop=c == FC - 1)
                    last.then_inc(ye_full, 1)

                def gathered(par, g):
                    pe.wait_ge(xe_full[par], g)

                def step(par, E, n, j, first, last, g):
                    gate_up(par, E, n, j, first)
                    if not last:
                        gathered(1 - par, g)
                        turn_xe(0, 1 - par, E + 1)
                    if not first:
                        down(1 - par, E - 1, n - 1, j, 0)
                    if not last:
                        turn_xe(1, 1 - par, E + 1)
                    if not first:
                        down(1 - par, E - 1, n - 1, j, 1)

                G0 = 16 * (NE // 2) * i
                gathered(0, G0 + 16)
                turn_xe(0, 0, N0)
                turn_xe(1, 0, N0)
                step(0, N0, L, 0, True, False, G0 + 16)
                step(1, N0 + 1, L + 3, 0, False, False, G0 + 32)
                step(0, N0 + 2, L + 6, 0, False, False, G0 + 32)
                with pe.Fori(1, NE // 2 - 1) as j:
                    step(1, 2 * j + (N0 + 1), L + 3, j, False, False, 16 * j + (G0 + 32))
                    step(0, 2 * j + (N0 + 2), L + 6, j, False, False, 16 * j + (G0 + 32))
                step(1, N0 + NE - 1, L + 3 * (NE - 1), 0, False, True, 0)
                turn_hidden(1, N0 + NE - 1)
                down(1, N0 + NE - 1, L + 3 * NE - 1, 0, 0)
                down(1, N0 + NE - 1, L + 3 * NE - 1, 0, 1)

            def window(i, w):
                _, loaded, step = ov[i, w][:3]
                own = L_PLE[i] + 3
                table_sums(step, step, 1)
                with pe.Fori(0, NE) as e:
                    def before(name):
                        pe.wait_ge(step, OV * e + (at[name] - 1))
                    before("xeT")
                    pe.wait_ge(loaded, 48 * e + 48)
                    pe.wait_ge(ov[i, w][6], 16 * e + 16)
                    for c in range(DC):
                        last = tr(bank[c // 4][:, (c % 4) * P:(c % 4 + 1) * P], xe[0][:, c::DC], ident[:, :])
                    last.then_inc(step, 1)
                    before("gu")
                    for k in range(2):
                        for c in range(DC):
                            last = mm(bank[2 + k][:, :], xeT[0][:, c, :], slot(own + k)[:, c * 512:(c + 1) * 512], start=c == 0, stop=c == DC - 1)
                    last.then_inc(step, 1)
                    before("hT")
                    for c in range(FC):
                        last = tr(bank[0][:, c * P:(c + 1) * P], hh[0][:, c::FC], ident[:, :])
                    last.then_inc(step, 1)
                    before("y")
                    for k in range(2):
                        for c in range(FC):
                            last = mm(bank[6 + k][:, :], hT[0][:, c * P:(c + 1) * P], slot(own + 2)[:, c * D + k * 512:c * D + (k + 1) * 512],
                                      start=c == 0, stop=c == FC - 1)
                    last.then_inc(step, 1)
                pe.wait_ge(step, OV * NE + OV_ROUTE)

            def ple_and_turn(i):
                def gate(t, n):
                    K = 8 * i + 2 * t + n
                    wait(pe, s_pg, K - 3)
                    ts = slice(t * P, (t + 1) * P)
                    pe.wait_ge(s_wlo, 20 + 3 * i + n + 2)
                    pe.wait_ge(s_xlo, 2 * NT * (i + 1) + 2 * t + 2)
                    hi, lo = ple_parts(i, n)
                    products = ((x_high, hi), (x_high, lo), (x_low_ple, hi))
                    for c in range(DC):
                        for k, (x_, w_) in enumerate(products):
                            last = mm(bank[2 + K % 4][:, :], x_[:, c, ts], w_[:, c, :], start=c == 0 and k == 0,
                                      stop=c == DC - 1 and k == len(products) - 1)
                    if t == 0:
                        last.then_inc(pg_full, 1)
                    else:
                        embed(t, n).then_inc(pg_full, 1)

                def embed(t, n):
                    K = 8 * i + 2 * t + n
                    w = slot(L_PLE[i] + 2)[:, 0:2048].rearrange("p (c n) -> p c n", c=2)
                    wait(pe, s_pp, K - 1)
                    for c in range(2):
                        last = mm(bank[6 + n][:, :], pT[:, c, t * P:(t + 1) * P], w[:, c, n * 512:(n + 1) * 512],
                                  start=c == 0, stop=c == 1)
                    return last

                weights(L_PLE[i] + 2)
                pe.wait_ge(ye_out, 2 * NE * (i + 1))
                for n in range(2):
                    embed(0, n)
                turn_normed(i, 1, 0)
                for t in range(NT + 1):
                    if t < NT:
                        xT_ready()
                        gate(t, 0)
                        if t + 1 < NT and t < 1:
                            turn_normed(i, 1, t + 1)
                        gate(t, 1)
                    if 1 <= t < NT - 1:
                        turn_normed(i, 1, t + 1)
                    if i + 1 < DEPTH and t == NT:
                        xT_ready()
                        pe.wait_ge(s_pg, 8 * i + 7)
                        qkv_sums(0)
                    if i + 1 < DEPTH and t >= 1:
                        pe.wait_ge(s_px, 8 * i + 2 * t)
                        pe.wait_ge(s_xlo, 2 * NT * (i + 1) + 2 * min(t + 2, NT))
                        turn_x(t - 1)

            def qkv_sums(t):
                for n in range(3):
                    K = 3 * t + n
                    w = weights(L_QKV + n)
                    wait(pe, qkv_out, K - 5)
                    for c in range(DC):
                        last = mm(bank[2 + K % 6][:, :], xT[:, c, t * P:(t + 1) * P], w[:, c, :], start=c == 0, stop=c == DC - 1)
                    last.then_inc(qkv_full, 1)

            def qkv():
                xT_ready()
                pe.wait_ge(s_px, 8)
                for t in range(1, NT + 1):
                    if t < NT:
                        qkv_sums(t)
                    if t >= 1:
                        pe.wait_ge(s_rot, t)
                        for a in range(3):
                            turn4(lambda k: rot[(t - 1) % 2][:, (4 * a + k) * P:(4 * a + k + 1) * P])

            def scores(u):
                b, kv = divmod(u, SWA_KV)
                wait(pe, sc_out, u - 1)
                lo = (b - 1) * P if b else 0
                for g in (0, 2, 1, 3):
                    h = GRP * kv + g
                    r = HD * (h % 2)
                    o = bank[2 + 2 * (u % 2) + g % 2][:, (g // 2) * 256 + (0 if b else P):(g // 2 + 1) * 256]
                    last = mm(o, qT1[r:r + HD, h // 2, b * P:(b + 1) * P], kT1[r:r + HD, kv, lo:(b + 1) * P], start=True, stop=True)
                last.then_inc(sc_full, 1)

            def swa():
                def turn_probs(u):
                    b = u // SWA_KV
                    pe.wait_ge(s_pr, u + 1)
                    pe.wait_ge(tr_out, n_tr[0])
                    wait(pe, pt_cur, u)
                    wait(pe, pt_prev, u - SWA_KV)
                    for j in (0, 1) if b else (1,):
                        for g in range(GRP):
                            last = tr(bank[j][:, g * P:(g + 1) * P], sc[u % 3][:, g, j * P:(j + 1) * P], ident[:, :])
                    last.then_inc(pt_full, 1)

                def weigh_v(u):
                    b, kv = divmod(u, SWA_KV)
                    js = (0, 1) if b else (1,)
                    pe.wait_ge(pt_cur, u + 1)
                    if b:
                        pe.wait_ge(pt_prev, u - SWA_KV + 1)
                    wait(pe, pv_out, u - 1)
                    for g in range(GRP):
                        for j in js:
                            last = mm(bank[6 + u % 2][:, g * HD:(g + 1) * HD], pT1[u % 2][:, j, g * P:(g + 1) * P],
                                      v1[:, b - 1 + j, kv * HD:(kv + 1) * HD], start=j == js[0], stop=j == 1)
                    last.then_inc(pv_full, 1)

                def turn_y(b, u):
                    pe.wait_ge(pv_out, SWA_KV * (b + 1))
                    pe.wait_ge(pt_cur, u)
                    pe.wait_ge(pt_prev, u - SWA_KV)
                    for a in range(2):
                        turn4(lambda k: y_sw[b % 2][:, (4 * a + k) * P:(4 * a + k + 1) * P])

                xT_ready()
                scores(0)
                scores(1)
                for u in range(UNITS + 2):
                    if u + 2 < UNITS:
                        scores(u + 2)
                    if u < UNITS:
                        turn_probs(u)
                    if u == UNITS:
                        pe.wait_ge(sc_out, UNITS)
                        pe.wait_ge(tr_out, n_tr[0])
                        out_proj(1, 0)
                    if 1 <= u <= UNITS:
                        weigh_v(u - 1)
                    if u == UNITS:
                        out_proj(1, 1)
                    if u >= 2 and (u - 2) % SWA_KV == SWA_KV - 1:
                        turn_y((u - 2) // SWA_KV, min(u + 1, UNITS))

            for i in range(DEPTH):
                if i == 1:
                    qkv()
                    swa()
                xT_ready()
                if i == 0:
                    pe.wait_ge(s_lru, 1)
                out_and_turn(i)
                router(i)
                experts(i)
                overflow(pe, i, window)
                ple_and_turn(i)

        @block.scalar
        def _(act):
            A = nc.scalar.activation
            n_tr, n_seq = [0], [0]

            def link(inst):
                inst.then_inc(s_act, 1)
                n_seq[0] += 1
                act.wait_ge(s_act, n_seq[0])

            def copy_out(dst, view="p (c s) -> p c s", **kw):
                n = n_tr[0]
                act.wait_ge(tr_full, n + 1)
                A(dst, bank[n % 2][:, :].rearrange(view, **kw), ACT.Copy).then_inc(tr_out, 1)
                n_tr[0] += 1

            def copy_x(t, to=xT):
                for a in range(2):
                    copy_out(to[:, 4 * a:4 * a + 4, t * P:(t + 1) * P], c=4)

            act.dma_start(pos_row, positions[0].rearrange("(t p) -> t p", p=P)).then_inc(s_posn, 16)
            for k, v in enumerate((conv_b, lru_b_r, lru_b_i, lru_lambda)):
                act.dma_start(rows[LC * k:LC * k + LC, :], v[0].rearrange("(c p) -> c p", p=P)).then_inc(s_small, 16)
            act.dma_start(rows[16:32, :], conv_w[0].rearrange("w (c p) -> (w c) p", p=P)).then_inc(s_small, 16)

            for t in range(NT):
                copy_x(t, x_high)
            act.wait_ge(tr_full, 2 * NT + 1)
            A(lru_p[:, 0:4, :], bank[0][:, 0:16].rearrange("p (k c) -> p k c", k=4), ACT.Copy)
            A(conv_p[:, :, :], bank[0][:, 16:32].rearrange("p (w c) -> p w c", w=4), ACT.Copy)
            A(route[:, 0:4], bank[0][:, 32:36], ACT.Copy).then_inc(tr_out, 1)
            n_tr[0] += 1

            def high(n):
                k, j = divmod(n, 4)
                if k == 0:
                    act.wait_ge(s_w0, 16 * 3)
                if k > 0 or j == 3:
                    act.wait_ge(in_full[k], 16)
                if k >= 2:
                    act.wait_ge(proj_full, 4 * (k - 1))
                b = slice(j * P, (j + 1) * P)
                A(rounded[3 + k % 2][:, :, b], w_raw(k)[:, :, b], ACT.Copy).then_inc(s_whi, 1)

            def small_functions():
                act.wait_ge(s_lrup, 1)
                A(lru_p[:, 5, :], lru_p[:, 5, :], ACT.Exp).then_inc(s_lrup, 1)
                act.wait_ge(s_ang, 2)
                A(cos_t[:, :, :], cos_t[:, :, :], ACT.Sin).then_inc(s_rope, 1)
                A(sin_t[:, 1, :, :], sin_t[:, 1, :, :], ACT.Sin).then_inc(s_rope, 1)

            for n in range(4):
                high(n)

            def z_copy(h):
                act.wait_ge(z_full, h + 1)
                wait(act, y_full, h - 2)
                for b, (o, n) in enumerate(((0, 512), (512, 512), (1024, 256))):
                    last = A(zb[h % 3][:, o:o + n], bank[2 + b][:, 0:n], ACT.Copy, scale=HD ** -0.5)
                last.then_inc(z_out, 1)

            def log1p_exp(h):
                act.wait_ge(s_neg, h + 1)
                link(A(tb[h % 2], tb[h % 2], ACT.Exp))
                A(tb[h % 2], tb[h % 2], ACT.Ln, bias=1.0).then_inc(s_ln1p, 1)

            for n in range(20):
                kind, j = n // 4, n % 4
                for m in split_at(n):
                    high(m)
                if n == 0:
                    small_functions()
                if n == 16:
                    act.wait_ge(s_u2, LC)
                    A(gi[:, :, :], gi[:, :, :], ACT.Sqrt, scale=-1.0).then_inc(s_sq, 1)
                act.wait_ge(proj_full, n + 1)
                dst = ((xr, gr, qT, kT, v0)[kind])[:, j, :]
                A(dst, bank[proj_bank(n)][:, :], ACT.Gelu_apprx_tanh if kind == 1 else ACT.Copy).then_inc(proj_out, 1)
                if n == 17:
                    act.wait_ge(s_lru, 1)
                if n in (17, 18):
                    z_copy(n - 17)
                    log1p_exp(n - 17)
                if n in (8, 10, 12, 14):
                    c = (n - 8) // 2
                    if c == 0:
                        act.wait_ge(s_lrup, 3)
                    act.wait_ge(gate_full, 2 * c + 1)
                    wait(act, s_u2, c)
                    A(r_t, bank[6][:, :], ACT.Tanh, scale=0.5, bias=lru_p[:, 1, c:c + 1]).then_inc(gate_out, 1)
                    act.wait_ge(gate_full, 2 * c + 2)
                    A(gi[:, c, :], bank[7][:, :], ACT.Tanh, scale=0.5, bias=lru_p[:, 2, c:c + 1]).then_inc(gate_out, 1)
                    act.wait_ge(gate_out, 2 * c + 1)
                    A(r_t, r_t, ACT.Tanh, scale=lru_p[:, 4, c:c + 1], bias=lru_p[:, 4, c:c + 1]).then_inc(s_T, 1)

            for h in range(SBH):
                if 2 <= h + 1 < SBH:
                    z_copy(h + 1)
                    log1p_exp(h + 1)
                act.wait_ge(s_arg, h + 1)
                A(zb[h % 3], zb[h % 3], ACT.Exp).then_inc(s_w, 1)

            def store_and_copy(i):
                for t in range(NT):
                    act.wait_ge(s_xln, 8 * i + t + 1)
                    act.dma_start(x_dram[i][t * P:(t + 1) * P, :], x_tok[:, t, :]).then_inc(s_xd, 16)
                    copy_x(t)

            def moe_loads(i):
                act.wait_ge(op_full, 8 * (i + 1))
                act.dma_start(p_tok, p[i, 0].rearrange("(t p) n -> p t n", p=P)).then_inc(s_p, 16)
                act.dma_start(vec_ffn[:, 0, :], ln_ffn_g[i].partition_broadcast(P)).then_inc(s_vffn, 16)
                act.dma_start(vec_ffn[:, 1, :], ln_ffn_b[i].partition_broadcast(P)).then_inc(s_vffn, 16)
                act.dma_start(b_ple, ple_b_gate[i].partition_broadcast(P)).then_inc(s_vffn, 16)
                if i + 1 < DEPTH:
                    act.wait_ge(s_xln, 8 * i + 4)
                    act.dma_start(vec_mix[:, 0, :], ln_mix_g[i + 1].partition_broadcast(P)).then_inc(s_vmix, 16)
                    act.dma_start(vec_mix[:, 1, :], ln_mix_b[i + 1].partition_broadcast(P)).then_inc(s_vmix, 16)

            def router(i):
                act.wait_ge(s_lg, i + 1)
                A(r_probs, r_probs, ACT.Exp).then_inc(s_ex, 1)
                for b in range(2):
                    copy_out(pT[:, :, b * 256:(b + 1) * 256], c=2)
                act.wait_ge(s_xd, 64 * (i + 1))
                for t in range(NT):
                    A(x_tok[:, t, :], x_tok[:, t, :], ACT.Copy, scale=ALPHA).then_inc(s_xa, 1)

            def experts(i):
                N0 = NE * i

                def tanh(par, E):
                    act.wait_ge(g_full, E + 1)
                    wait(act, s_h, E - 1)
                    A(th[par], bank[2 + 2 * par][:, :], ACT.Tanh, scale=0.5).then_inc(s_th, 1)

                def xe_copy(half, par, E):
                    act.wait_ge((xa_full, xb_full)[half], E + 1)
                    A(xeT[par][:, 4 * half:4 * half + 4, :], bank[1 - half][:, :].rearrange("p (c s) -> p c s", c=4), ACT.Copy)\
                        .then_inc((xa_out, xb_out)[half], 1)

                def y_copy(half, par, E, wr):
                    act.wait_ge(ye_full, 2 * E + 1 + half)
                    if half == 0:
                        wait(act, y_wr[par], wr)
                    A(yy[par][:, half * 512:(half + 1) * 512], bank[6 + half][:, :], ACT.Copy).then_inc(ye_out, 1)

                def y_store(par, e, E):
                    act.wait_ge(ye_out, 2 * E + 2)
                    dst = y_dram[i][0][e * P:(e + 1) * P, :] if isinstance(e, int) else y_dram[i][0][bass.ds(e * P, P), :]
                    act.dma_start(dst, yy[par]).then_inc(y_wr[par], 16)

                def step(par, e, E, first, last, wr):
                    tanh(par, E)
                    if not last:
                        xe_copy(0, 1 - par, E + 1)
                    if not first:
                        y_copy(0, 1 - par, E - 1, wr)
                    if not last:
                        xe_copy(1, 1 - par, E + 1)
                    if not first:
                        y_copy(1, 1 - par, E - 1, wr)
                        y_store(1 - par, e - 1, E - 1)

                W0 = 16 * (NE // 2) * i
                xe_copy(0, 0, N0)
                xe_copy(1, 0, N0)
                step(0, 0, N0, True, False, 0)
                step(1, 1, N0 + 1, False, False, W0)
                step(0, 2, N0 + 2, False, False, W0)
                with act.Fori(1, NE // 2 - 1) as j:
                    step(1, 2 * j + 1, 2 * j + (N0 + 1), False, False, 16 * j + W0)
                    step(0, 2 * j + 2, 2 * j + (N0 + 2), False, False, 16 * j + W0)
                step(1, NE - 1, N0 + NE - 1, False, True, W0 + 16 * (NE // 2 - 1))
                y_copy(0, 1, N0 + NE - 1, W0 + 16 * (NE // 2 - 1))
                y_copy(1, 1, N0 + NE - 1, 0)
                y_store(1, NE - 1, N0 + NE - 1)

            def window(i, w):
                step, written = ov[i, w][2:4]

                def expert(e, peeled):
                    def before(name):
                        act.wait_ge(step, e * OV + (at[name] - 1))
                    before("xeT_out")
                    for k in range(2):
                        last = A(xeT[0][:, 4 * k:4 * k + 4, :], bank[k][:, :].rearrange("p (c s) -> p c s", c=4), ACT.Copy)
                    last.then_inc(step, 1)
                    before("tanh")
                    A(th[0], bank[2][:, :], ACT.Tanh, scale=0.5).then_inc(step, 1)
                    before("y_out")
                    if not peeled:
                        act.wait_ge(written, e * 16)
                    for k in range(2):
                        last = A(yy[0][:, k * 512:(k + 1) * 512], bank[6 + k][:, :], ACT.Copy)
                    last.then_inc(step, 1)
                    act.wait_ge(step, e * OV + at["y_out"])
                    dst = y_dram[i][w][0:P, :] if peeled else y_dram[i][w][bass.ds(e * P, P), :]
                    act.dma_start(dst, yy[0]).then_inc(written, 16)
                expert(0, True)
                with act.Fori(1, NE) as e:
                    expert(e, False)
                act.wait_ge(written, 16 * NE)

            def ple(i):
                def tanh(k):
                    act.wait_ge(s_pg, 8 * i + k + 1)
                    A(gt[k % 2], gt[k % 2], ACT.Tanh, scale=0.5).then_inc(s_pt, 1)

                def after(t):
                    if i + 1 < DEPTH:
                        copy_x(t)
                    else:
                        act.wait_ge(s_px, 8 * i + 2 * t + 2)
                        act.dma_start(out[0, t * P:(t + 1) * P, :], x_tok[:, t, :]).then_inc(s_out, 16)

                for n in range(2):
                    act.wait_ge(ring_full[(L_PLE[i] + n) % SLOTS], 16 * ring_times(L_PLE[i] + n))
                    A(ple_parts(i, n)[0][:, :, :], ple_raw(i, n), ACT.Copy).then_inc(s_whi, 1)
                copy_x(0, x_high)
                copy_x(1, x_high)
                for t in range(NT):
                    tanh(2 * t)
                    tanh(2 * t + 1)
                    if t + 2 < NT:
                        copy_x(t + 2, x_high)
                    after(t)

            def qkv():
                for t in range(NT + 1):
                    if t < NT:
                        wait(act, s_rot, t - 1)
                        for n in range(3):
                            K = 3 * t + n
                            act.wait_ge(qkv_full, K + 1)
                            b = bank[2 + K % 6]
                            if n < 2:
                                A(raw[t % 2][:, n * 512:(n + 1) * 512], b[:, :], ACT.Copy).then_inc(qkv_out, 1)
                            else:
                                A(raw[t % 2][:, 1024:1280], b[:, 0:256], ACT.Copy)
                                A(v1[:, t, :], b[:, 256:512], ACT.Copy).then_inc(qkv_out, 1)
                    if t >= 1:
                        ts = slice((t - 1) * P, t * P)
                        copy_out(qT1[:, 0:4, ts], c=4)
                        copy_out(qT1[:, 4:8, ts], c=4)
                        copy_out(kT1[:, :, ts], c=4)

            def swa():
                def probs(u):
                    b = u // SWA_KV
                    act.wait_ge(s_nm, u + 1)
                    lo = 0 if b else P
                    m = sm[:, u % 4, :]
                    for g in range(GRP):
                        A(sc[u % 3][:, g, lo:], sc[u % 3][:, g, lo:], ACT.Exp, bias=m[:, 4 + g:5 + g], accum_out=m[:, 8 + g:9 + g])
                    A(m[:, 12:16], m[:, 12:16], ACT.Exp).then_inc(s_pr, 1)

                probs(0)
                probs(1)
                for u in range(UNITS + 2):
                    if u < UNITS:
                        act.wait_ge(pt_full, u + 1)
                        wait(act, pv_full, u - 1)
                        if u >= SWA_KV:
                            A(pT1[u % 2][:, 0, :], bank[0][:, :], ACT.Copy).then_inc(pt_prev, 1)
                        A(pT1[u % 2][:, 1, :], bank[1][:, :], ACT.Copy).then_inc(pt_cur, 1)
                    if u + 2 < UNITS:
                        probs(u + 2)
                    if u >= 2 and (u - 2) % SWA_KV == SWA_KV - 1:
                        b = (u - 2) // SWA_KV
                        for a in range(2):
                            copy_out(xT[:, 4 * a:4 * a + 4, b * P:(b + 1) * P], c=4)

            for i in range(DEPTH):
                if i == 1:
                    qkv()
                    swa()
                store_and_copy(i)
                moe_loads(i)
                router(i)
                experts(i)
                overflow(act, i, window, y_wr)
                ple(i)
            act.wait_ge(s_out, 16 * NT)

        @block.vector
        def _(dve):
            V = nc.vector
            n_seq = [0]

            def link(inst):
                inst.then_inc(s_dve, 1)
                n_seq[0] += 1
                dve.wait_ge(s_dve, n_seq[0])

            dve.wait_ge(s_posn, 16)
            V.tensor_copy(rows[32:36, :], pos_row).then_inc(s_posf, 1)

            def x_low(g):
                t, a = divmod(g, 2)
                at_ = (slice(None), slice(4 * a, 4 * a + 4), slice(t * P, (t + 1) * P))
                dve.wait_ge(tr_out, g + 1)
                V.tensor_tensor(rounded[5][at_], bank[g % 2][:, :].rearrange("p (c s) -> p c s", c=4), x_high[at_].bitcast(F32),
                                ALU.subtract).then_inc(s_xlo, 1)

            def low(n):
                k, b = n // 4, slice(n % 4 * P, (n % 4 + 1) * P)
                dve.wait_ge(s_whi, n + 1)
                V.tensor_tensor(rounded[k % 3][:, :, b], w_raw(k)[:, :, b], rounded[3 + k % 2][:, :, b].bitcast(F32), ALU.subtract).then_inc(s_wlo, 1)

            for g in range(2 * NT):
                x_low(g)
            for n in range(4):
                low(n)
            dve.wait_ge(tr_out, 2 * NT + 1)
            nl, e, s, q, acc = (lru_p[:, k, :] for k in (3, 5, 6, 7, 4))
            link(V.tensor_scalar(nl, nl, -1.0, None, ALU.mult))
            link(V.scalar_tensor_tensor(e, nl, -1.0, nl, ALU.mult, ALU.min))
            V.tensor_scalar(lru_p[:, 1:3, :], lru_p[:, 1:3, :], 0.5, None, ALU.mult).then_inc(s_lrup, 1)
            dve.wait_ge(s_const, 2)
            pos_f, frq = route[:, 0:4], band[:, 0:32]
            ang = route[:, 64:192].rearrange("p (t f) -> p t f", t=NT)
            link(V.tensor_tensor(ang, pos_f.unsqueeze(2).to_broadcast([P, NT, 32]),
                                 frq.unsqueeze(1).to_broadcast([P, NT, 32]), ALU.mult))
            turns_f = sin_t[:, 0, :, :]
            for dst, quarter in ((cos_t[:, :, :], 0.25), (sin_t[:, 1, :, :], 0.0)):
                link(V.tensor_scalar(dst, ang, 1 / TWO_PI, quarter, ALU.mult, ALU.add))
                link(V.tensor_copy(turns_i, dst))
                link(V.tensor_copy(turns_f, turns_i))
                link(V.scalar_tensor_tensor(dst, turns_f, -TURN[0], ang, ALU.mult, ALU.add))
                for part in TURN[1:]:
                    link(V.scalar_tensor_tensor(dst, turns_f, -part, dst, ALU.mult, ALU.add))
                link(V.tensor_scalar(dst, dst, quarter * TWO_PI, PI, ALU.add, ALU.min))
                V.tensor_scalar(dst, dst, -PI, None, ALU.max).then_inc(s_ang, 1)
            dve.wait_ge(s_lrup, 2)
            link(V.tensor_scalar(s, e, 2.0, None, ALU.add))
            link(V.reciprocal(s, s))
            link(V.tensor_tensor(s, s, e, ALU.mult))
            link(V.tensor_tensor(q, s, s, ALU.mult))
            link(V.tensor_scalar(acc, q, 1 / 17, 1 / 15, ALU.mult, ALU.add))
            for k in (13, 11, 9, 7, 5, 3, 1):
                link(V.tensor_tensor(acc, acc, q, ALU.mult))
                link(V.tensor_scalar(acc, acc, 1 / k, None, ALU.add))
            link(V.tensor_tensor(acc, acc, s, ALU.mult))
            link(V.tensor_scalar(nl, nl, 0.0, 2.0, ALU.max, ALU.mult))
            V.scalar_tensor_tensor(acc, acc, 4.0, nl, ALU.mult, ALU.add).then_inc(s_lrup, 1)

            def conv(c):
                dve.wait_ge(proj_out, c + 1)
                link(V.tensor_scalar(xc[:, c, :], xr[:, c, :], conv_p[:, 3, c:c + 1], lru_p[:, 0, c:c + 1], ALU.mult, ALU.add))
                for d in (1, 2, 3):
                    last = V.scalar_tensor_tensor(xc[:, c, d:], xr[:, c, :S - d], conv_p[:, 3 - d, c:c + 1], xc[:, c, d:], ALU.mult, ALU.add)
                    if d < 3:
                        link(last)
                last.then_inc(s_conv, 1)

            def decay(c):
                dve.wait_ge(s_T, c + 1)
                link(V.tensor_scalar(r_d, r_t, 1.0, None, ALU.add))
                link(V.reciprocal(r_d, r_d))
                link(V.scalar_tensor_tensor(r_t, r_t, 2.0, r_d, ALU.mult, ALU.mult))
                V.tensor_scalar(xr[:, c, :], r_t, -1.0, 1.0, ALU.mult, ALU.add)
                link(V.scalar_tensor_tensor(xc[:, c, :], gi[:, c, :], 1.0, xc[:, c, :], ALU.add, ALU.mult))
                V.scalar_tensor_tensor(gi[:, c, :], r_t, 2.0, r_t, ALU.subtract, ALU.mult).then_inc(s_u2, 1)

            for n in range(16):
                for m in split_at(n):
                    low(m)
                if 1 <= n < 1 + LC:
                    conv(n - 1)
                if n in (9, 11, 13, 15):
                    decay((n - 9) // 2)
            dve.wait_ge(s_sq, 1)
            link(V.scalar_tensor_tensor(xc[:, :, :], xc[:, :, :], 0.5, gi[:, :, :], ALU.mult, ALU.mult))
            for c in range(LC):
                last = V.tensor_tensor_scan(gi[:, c, :], xr[:, c, :], xc[:, c, :], 0.0, ALU.mult, ALU.add)
            link(last)
            dve.wait_ge(proj_out, 8)
            V.tensor_tensor(gr[:, :, :], gr[:, :, :], gi[:, :, :], ALU.mult).then_inc(s_lru, 1)

            def softplus(h):
                z, t = zb[h % 3], tb[h % 2]
                dve.wait_ge(z_out, h + 1)
                wait(dve, c_full, h - 1)
                V.scalar_tensor_tensor(t, z, -1.0, z, ALU.mult, ALU.min).then_inc(s_neg, 1)
                dve.wait_ge(s_ln1p, h + 1)
                V.scalar_tensor_tensor(t, z, 0.0, t, ALU.max, ALU.add).then_inc(s_sp, 1)

            def argument(h):
                dve.wait_ge(c_full, h + 1)
                for b, (o, n) in enumerate(((0, 512), (512, 512), (1024, 256))):
                    last = V.tensor_tensor(zb[h % 3][:, o:o + n], bank[5 + b][:, 0:n], zb[h % 3][:, o:o + n], ALU.add)
                last.then_inc(s_arg, 1)

            def y_copy(h):
                dve.wait_ge(y_full, h + 1)
                r = HD * (h % 2)
                V.tensor_copy(xT[r:r + HD, h // 2, :], bank[h % 2][r:r + HD, :]).then_inc(y_out, 1)

            softplus(0)
            for h in range(SBH + 1):
                if h + 1 < SBH:
                    softplus(h + 1)
                if h < SBH:
                    argument(h)
                if h >= 1:
                    y_copy(h - 1)

            def ln_stats(i, kind, t):
                for k in range(2):
                    last = V.bn_stats(st[:, t, k, :], x_tok[:, t, k * 512:(k + 1) * 512])
                link(last)
                link(V.bn_aggr(mv[:, t, :], st[:, t, :, :]))
                V.tensor_scalar(lnp[:, t, 0:1], mv[:, t, 1:2], EPS, None, ALU.add).then_inc(s_ve, 1)

            def ln_scale(i, kind, t, g, b):
                K = 4 * (2 * i + kind) + t + 1
                V.scalar_tensor_tensor(x_tok[:, t, :], x_tok[:, t, :], mv[:, t, 0:1], g, ALU.subtract, ALU.mult).then_inc(s_xc, 1)
                dve.wait_ge(s_xc, K)
                dve.wait_ge(s_rstd, K)
                V.scalar_tensor_tensor(x_tok[:, t, :], x_tok[:, t, :], lnp[:, t, 1:2], b, ALU.mult, ALU.add).then_inc(s_xln, 1)

            def add_and_norm(i):
                dve.wait_ge(s_vmix, 32 * (i + 1))
                for t in range(NT):
                    for n in range(2):
                        K = 8 * i + 2 * t + n
                        dve.wait_ge(op_full, K + 1)
                        xs = x_tok[:, t, n * 512:(n + 1) * 512]
                        last = V.scalar_tensor_tensor(xs, xs, ALPHA, bank[2 + K % 4][:, :], ALU.mult, ALU.add).then_inc(op_out, 1)
                    dve.wait_ge(op_out, 8 * i + 2 * t + 2)
                    ln_stats(i, 0, t)
                    ln_scale(i, 0, t, vec_mix[:, 0, :], vec_mix[:, 1, :])

            def one_hots(w, link=link):
                link(V.tensor_scalar(rwin[:, :, :], rsel[:, :, :], float(-w * P), None, ALU.add))
                for t in range(NT):
                    last = V.tensor_tensor(onehot[t], places, rwin[:, t, :].unsqueeze(1).to_broadcast([P, P, NE]), ALU.is_equal)
                return last

            def table(link=link):
                sums = bank[4][:, 0:2 * NE].rearrange("p (e k) -> p e k", k=2)
                link(V.tensor_copy(route[:, 192:224], bank[4][:, 0:2 * NE]))
                two = route[:, 192:224].rearrange("p (e k) -> p e k", k=2)
                return V.tensor_tensor(idx_i[:, :], two[:, :, 0], two[:, :, 1], ALU.add)

            def router(i):
                off = [14336 + 64]

                def tmp(n):
                    off[0] += n
                    return work[:, off[0] - n:off[0]]
                pr = r_probs
                te = pr.rearrange("p (t e) -> p t e", t=NT)
                gx = pr.rearrange("p (g x) -> p g x", x=GS)
                t1, c1, oh1, oh2, pr2, rk = (tmp(64) for _ in range(6))
                v3 = lambda a: a.rearrange("p (g x) -> p g x", x=GS)
                t3 = lambda a: a.rearrange("p (t e) -> p t e", t=NT)
                g1, g2, mk, gsum, geq, ohg, m1, m2 = (tmp(16) for _ in range(8))
                gm, p1, p2, den = (tmp(4) for _ in range(4))
                over = lambda a, n: a.unsqueeze(2).to_broadcast([P, a.shape[1], n])
                key = key4[:, :].unsqueeze(1).to_broadcast([P, NT * NG, GS])
                key_g = key4[:, :].unsqueeze(1).to_broadcast([P, NT, NG])

                def first_max(src3, mx, oh3, t3_, c3, mk_, n, key_):
                    link(V.tensor_reduce(mx, src3, AX.X, ALU.max))
                    link(V.tensor_tensor(t3_, src3, over(mx, n), ALU.is_equal))
                    link(V.tensor_tensor(c3, t3_, key_, ALU.mult))
                    link(V.tensor_reduce(mk_, c3, AX.X, ALU.max))
                    link(V.tensor_tensor(oh3, c3, over(mk_, n), ALU.is_equal))

                dve.wait_ge(lg_full, i + 1)
                link(V.tensor_tensor(te, bank[6][:, 0:NT * NE].rearrange("p (t e) -> p t e", t=NT),
                                     b_rt[:, :].unsqueeze(1).to_broadcast([P, NT, NE]), ALU.add))
                link(V.tensor_reduce(gm, te, AX.X, ALU.max))
                V.tensor_tensor(te, te, over(gm, NE), ALU.subtract).then_inc(s_lg, 1)
                dve.wait_ge(s_ex, i + 1)
                link(V.tensor_reduce(den, te, AX.X, ALU.add))
                link(V.reciprocal(den, den))
                link(V.tensor_tensor(te, te, over(den, NE), ALU.mult))
                first_max(gx, g1, v3(oh1), v3(t1), v3(c1), mk, GS, key)
                link(V.scalar_tensor_tensor(pr2, oh1, -4.0, pr, ALU.mult, ALU.add))
                first_max(v3(pr2), g2, v3(oh2), v3(t1), v3(c1), mk, GS, key)
                link(V.tensor_tensor(gsum, g1, g2, ALU.add))
                first_max(v3(gsum), gm, v3(ohg), v3(geq), v3(m1), p1, NG, key_g)
                V.tensor_tensor(v3(oh1), v3(oh1), over(ohg, GS), ALU.mult)
                V.tensor_tensor(m1, g1, ohg, ALU.mult)
                link(V.tensor_tensor(v3(oh2), v3(oh2), over(ohg, GS), ALU.mult))
                V.tensor_tensor(m2, g2, ohg, ALU.mult)
                V.tensor_tensor(mask_bf[:, :, :], t3(oh1), t3(oh2), ALU.add).then_inc(s_mask, 1)
                link(V.tensor_tensor(c1, oh1, oh2, ALU.add))
                dve.wait_ge(rk_full, i + 1)
                link(V.scalar_tensor_tensor(rsel, t3(bank[7][:, 0:64]), 1.0, t3(c1), ALU.add, ALU.mult))
                link(V.tensor_scalar(rsel, rsel, 1.0, None, ALU.subtract))
                dve.wait_ge(s_const, 4)
                one_hots(0).then_inc(s_onehot, 1)
                dve.wait_ge(id_full, i + 1)
                table().then_inc(s_idx, 1)
                link(V.tensor_copy(rk, bank[7][:, 0:64]))
                link(V.tensor_reduce(p1, v3(m1), AX.X, ALU.add))
                link(V.tensor_reduce(p2, v3(m2), AX.X, ALU.add))
                link(V.tensor_tensor(den, p1, p2, ALU.add))
                link(V.reciprocal(den, den))
                V.tensor_tensor(wgt[:, 0, :], p1, den, ALU.mult)
                link(V.tensor_tensor(wgt[:, 1, :], p2, den, ALU.mult))
                link(V.tensor_reduce(m1[:, 0:1], bank[7][:, 64:80], AX.X, ALU.max))
                V.tensor_copy(most_i[:, :], m1[:, 0:1]).then_inc(s_most, 1)
                link(V.tensor_tensor(t3(t1), t3(rk), e_base[:, :].unsqueeze(1).to_broadcast([P, NT, NE]), ALU.add))
                for w in range(1, WINDOWS):
                    link(V.tensor_scalar(pr2, rk, float(w * P), float((NE - 1) * P), ALU.is_ge, ALU.mult))
                    link(V.tensor_tensor(t1, t1, pr2, ALU.add))
                for k, oh in enumerate((oh1, oh2)):
                    link(V.tensor_tensor(pr2, t1, oh, ALU.mult))
                    link(V.tensor_reduce(p1, t3(pr2), AX.X, ALU.add))
                    link(V.tensor_copy(pos_i[:, 0, k, :], p1))
                    for w in range(1, WINDOWS):
                        link(V.tensor_scalar(p1, p1, float(-NE * P), None, ALU.add))
                        link(V.tensor_scalar(p2, p1, 0.0, float(8 * NE * P), ALU.is_lt, ALU.mult))
                        link(V.tensor_tensor(pos_i[:, w, k, :], p1, p2, ALU.add))

            def experts(i):
                N0 = NE * i

                def hT_copy(par, E):
                    dve.wait_ge(ht_full, E + 1)
                    V.tensor_copy(hT[par], bank[0][:, :]).then_inc(ht_out, 1)

                def hidden(par, E):
                    dve.wait_ge(s_th, E + 1)
                    V.scalar_tensor_tensor(th[par], th[par], 1.0, bank[2 + 2 * par][:, :], ALU.add, ALU.mult).then_inc(s_hg, 1)
                    dve.wait_ge(s_hg, E + 1)
                    dve.wait_ge(u_full, E + 1)
                    V.scalar_tensor_tensor(hh[par], th[par], 0.5, bank[3 + 2 * par][:, :], ALU.mult, ALU.mult).then_inc(s_h, 1)

                hidden(0, N0)
                with dve.Fori(0, NE // 2 - 1) as j:
                    hT_copy(0, 2 * j + N0)
                    hidden(1, 2 * j + (N0 + 1))
                    hT_copy(1, 2 * j + (N0 + 1))
                    hidden(0, 2 * j + (N0 + 2))
                hT_copy(0, N0 + NE - 2)
                hidden(1, N0 + NE - 1)
                hT_copy(1, N0 + NE - 1)

            def window(i, w):
                step, own = ov[i, w][2], ov[i, w][4]

                def link_1(inst):
                    inst.then_inc(own, 1)
                    dve.wait_ge(own, 1)

                def link_2(inst):
                    inst.then_inc(own, 1)
                    dve.wait_ge(own, 2)
                one_hots(w, link_1).then_inc(step, 1)
                dve.wait_ge(step, 2)
                table(link_2).then_inc(step, 1)
                with dve.Fori(0, NE) as e:
                    def before(name):
                        dve.wait_ge(step, e * OV + (at[name] - 1))
                    before("silu")
                    V.scalar_tensor_tensor(th[0], th[0], 1.0, bank[2][:, :], ALU.add, ALU.mult).then_inc(step, 1)
                    before("h")
                    V.scalar_tensor_tensor(hh[0], th[0], 0.5, bank[3][:, :], ALU.mult, ALU.mult).then_inc(step, 1)
                    before("hT_out")
                    V.tensor_copy(hT[0], bank[0][:, :]).then_inc(step, 1)
                dve.wait_ge(step, OV * NE + OV_ROUTE)

            def combine_and_ple(i):
                dve.wait_ge(s_vffn, 48 * (i + 1))

                def combine(t):
                    y = yg[t % 2]
                    dve.wait_ge(s_xa, NT * i + t + 1)
                    dve.wait_ge(s_yg[t % 2], 32 * (2 * i + t // 2 + 1))
                    link(V.scalar_tensor_tensor(x_tok[:, t, :], y[:, 0, :], wgt[:, 0, t:t + 1], x_tok[:, t, :], ALU.mult, ALU.add))
                    V.scalar_tensor_tensor(x_tok[:, t, :], y[:, 1, :], wgt[:, 1, t:t + 1], x_tok[:, t, :], ALU.mult, ALU.add).then_inc(s_comb, 1)
                    dve.wait_ge(s_comb, NT * i + t + 1)
                    ln_stats(i, 1, t)
                    ln_scale(i, 1, t, vec_ffn[:, 0, :], vec_ffn[:, 1, :])

                def biased(t, n):
                    K = 8 * i + 2 * t + n
                    dve.wait_ge(pg_full, K + 1)
                    wait(dve, s_px, K - 1)
                    V.tensor_tensor(gt[n], bank[2 + K % 4][:, :], b_ple[:, n * 512:(n + 1) * 512], ALU.add).then_inc(s_pg, 1)

                def gated(t, n):
                    K = 8 * i + 2 * t + n
                    dve.wait_ge(s_pt, K + 1)
                    V.scalar_tensor_tensor(gt[n], gt[n], 1.0, bank[6 + n][:, :], ALU.add, ALU.mult).then_inc(s_pp, 1)
                    dve.wait_ge(s_pp, K + 1)
                    xs = x_tok[:, t, n * 512:(n + 1) * 512]
                    return V.scalar_tensor_tensor(xs, gt[n], 0.5, xs, ALU.mult, ALU.add).then_inc(s_px, 1)

                def weights_low(n):
                    dve.wait_ge(s_whi, 20 + 2 * i + n + 1)
                    if n == 1:
                        dve.wait_ge(s_wlo, 20 + 3 * i + 2)
                    cs = slice(0 if n else DC // 2, DC)
                    hi, lo = ple_parts(i, n)
                    V.tensor_tensor(lo[:, cs, :], ple_raw(i, n)[:, cs, :], hi[:, cs, :].bitcast(F32), ALU.subtract).then_inc(s_wlo, 1)

                def tile_low(t):
                    for a in range(2):
                        g = TR_PLE[i] + 2 * t + a + (2 if i == 0 and t == NT - 1 else 0)
                        at_ = (slice(None), slice(4 * a, 4 * a + 4), slice(t * P, (t + 1) * P))
                        dve.wait_ge(tr_out, g + 1)
                        V.tensor_tensor(x_low_ple[at_], bank[g % 2][:, :].rearrange("p (c s) -> p c s", c=4),
                                        x_high[at_].bitcast(F32), ALU.subtract).then_inc(s_xlo, 1)

                weights_low(0)
                combine(0)
                tile_low(0)
                combine(1)
                weights_low(1)
                tile_low(1)
                for t in range(NT):
                    biased(t, 0)
                    biased(t, 1)
                    gated(t, 0)
                    gated(t, 1)
                    if t + 2 < NT:
                        combine(t + 2)
                        tile_low(t + 2)

            def qkv():
                dve.wait_ge(s_rope, 3)
                for t in range(NT):
                    r = raw[t % 2]
                    dve.wait_ge(qkv_out, 3 * t + 3)
                    if t >= 2:
                        dve.wait_ge(tr_full, TR_QKV + 3 * (t - 1))
                    link(V.tensor_tensor(rope_a.rearrange("p (h f) -> p h f", f=32), r.rearrange("p (h f) -> p h f", f=32),
                                         cos_t[:, t, :].unsqueeze(1).to_broadcast([P, 40, 32]), ALU.mult))
                    dve.wait_ge(s_ropeb, t + 1)
                    V.tensor_tensor(rot[t % 2][:, 0:1024], rope_a[:, 0:1024], rope_b[:, 0:1024], ALU.add)
                    kd = rot[t % 2][:, 1024:1536].rearrange("p (k two d) -> p k two d", k=SWA_KV, two=2)
                    for c in range(2):
                        last = V.tensor_tensor(kd[:, :, c, :], rope_a[:, 1024:1280].rearrange("p (k d) -> p k d", d=HD),
                                               rope_b[:, 1024:1280].rearrange("p (k d) -> p k d", d=HD), ALU.add)
                    last.then_inc(s_rot, 1)
                    dve.wait_ge(s_rot, t + 1)

            def swa():
                def softmax_in(u):
                    b, kv = divmod(u, SWA_KV)
                    lo = 0 if b else P
                    s_, m = sc[u % 3], sm[:, u % 4, :]
                    dve.wait_ge(sc_full, u + 1)
                    wait(dve, pt_full, u - 2)
                    for k in range(2):
                        src = bank[2 + 2 * (u % 2) + k][:, :].rearrange("p (h s) -> p h s", h=2)
                        last = V.scalar_tensor_tensor(s_[:, k::2, lo:], src[:, :, lo:], HD ** -0.5,
                                                      band[:, lo:].unsqueeze(1).to_broadcast([P, 2, 2 * P - lo]), ALU.mult, ALU.add)
                    last.then_inc(sc_out, 1)
                    dve.wait_ge(sc_out, u + 1)
                    link(V.tensor_reduce(m[:, 0:4], s_[:, :, lo:], AX.X, ALU.max))
                    link(V.tensor_tensor(m[:, 0:4], m[:, 0:4], sinks[:, GRP * kv:GRP * (kv + 1)], ALU.max))
                    V.tensor_scalar(m[:, 4:8], m[:, 0:4], -1.0, None, ALU.mult)
                    V.tensor_tensor(m[:, 12:16], sinks[:, GRP * kv:GRP * (kv + 1)], m[:, 0:4], ALU.subtract).then_inc(s_nm, 1)

                def normed(u):
                    b, kv = divmod(u, SWA_KV)
                    m = sm[:, u % 4, :]
                    dve.wait_ge(s_pr, u + 1)
                    link(V.tensor_tensor(m[:, 16:20], m[:, 8:12], m[:, 12:16], ALU.add))
                    link(V.reciprocal(m[:, 16:20], m[:, 16:20]))
                    dve.wait_ge(pv_full, u + 1)
                    if kv == 0 and b >= 2:
                        dve.wait_ge(tr_full, TR_SWA + 2 * (b - 1))
                    V.tensor_tensor(y_sw[b % 2][:, kv * 256:(kv + 1) * 256].rearrange("p (h d) -> p h d", h=GRP),
                                         bank[6 + u % 2][:, 0:256].rearrange("p (h d) -> p h d", h=GRP),
                                         m[:, 16:20].unsqueeze(2).to_broadcast([P, GRP, HD]), ALU.mult).then_inc(pv_out, 1)

                softmax_in(0)
                softmax_in(1)
                for u in range(UNITS + 1):
                    if u + 2 < UNITS:
                        softmax_in(u + 2)
                    if u >= 1:
                        normed(u - 1)

            for i in range(DEPTH):
                if i == 1:
                    qkv()
                    swa()
                add_and_norm(i)
                router(i)
                experts(i)
                overflow(dve, i, window)
                combine_and_ple(i)

        @block.gpsimd
        def _(pool):
            G = nc.gpsimd
            n_seq = [0]

            def link(inst):
                inst.then_inc(s_pool, 1)
                n_seq[0] += 1
                pool.wait_ge(s_pool, n_seq[0])

            def select(ap, op, fill, base, pattern, mult):
                return G.affine_select(out=ap, in_=ap, pattern=pattern, compare_op=op, fill=fill, base=base, channel_multiplier=mult)

            link(G.memset(ident[:, :], 0.0))
            select(ident[:, :], ALU.not_equal, 1.0, 0, [[-1, P]], 1).then_inc(s_ident, 1)
            G.memset(w_bd[:, :, :, :], 0.0).then_inc(s_const, 1)
            for f in range(32):
                last = G.memset(band[:, f:f + 1], 10000.0 ** (-f / 32))
            last.then_inc(s_const, 1)
            G.memset(neg_tri[:, :], -1.0)
            G.memset(neg_ones[:, :], -1.0)
            G.memset(stri_bf[:, :], 1.0)
            G.memset(ones_bf[:, :], 1.0)
            G.memset(mhalf[:, :], -0.5)
            for k in range(4):
                G.memset(key4[:, k:k + 1], float(4 - k))
            link(G.iota(slot_i, pattern=[[1, P]], base=0, channel_multiplier=0))
            link(G.tensor_copy(slots_bf[:, :], slot_i))
            link(G.iota(slot_i[:, 0:NE], pattern=[[P, NE]], base=0, channel_multiplier=0))
            link(G.tensor_copy(e_base[:, :], slot_i[:, 0:NE]))
            link(G.iota(slot_i[:, 0:NT], pattern=[[0, NT]], base=0, channel_multiplier=1))
            link(G.tensor_copy(tok_id[:, :, 0], slot_i[:, 0:NT]))
            link(G.iota(slot_i[:, 0:NT], pattern=[[P, NT]], base=0, channel_multiplier=0))
            link(G.tensor_copy(tok_id[:, :, 1], slot_i[:, 0:NT]))
            select(neg_tri[:, :], ALU.is_ge, 0.0, 0, [[-1, P]], 1)
            select(stri_bf[:, :], ALU.is_gt, 0.0, 0, [[1, P]], -1).then_inc(s_const, 1)
            pool.wait_ge(s_rope, 2)
            link(G.memset(band[:, :], 0.0))
            link(select(band[:, :], ALU.is_ge, NEG, P, [[-1, 2 * P]], 1))
            link(select(band[:, :], ALU.is_gt, NEG, 0, [[1, 2 * P]], -1))
            G.tensor_scalar(sin_t[:, 0, :, :], sin_t[:, 1, :, :], -1.0, None, ALU.mult).then_inc(s_rope, 1)

            pool.wait_ge(gate_full, 2 * LC)
            G.tensor_copy(places, slots_bf[:, :].unsqueeze(2).to_broadcast([P, P, NE])).then_inc(s_const, 1)

            def mask(t, done):
                for kt in range(NT):
                    last = select(t[:, SEG[kt]:SEG[kt] + P], ALU.is_gt, 0.0, 0, [[1, P]], -1)
                last.then_inc(done, 1)

            def softplus_mask(h):
                pool.wait_ge(s_sp, h + 1)
                mask(tb[h % 2], s_spm)

            softplus_mask(0)
            for h in range(SBH):
                if h + 1 < SBH:
                    softplus_mask(h + 1)
                pool.wait_ge(s_w, h + 1)
                mask(zb[h % 3], s_wm)

            def inverse_root(i, kind, t):
                K = 4 * (2 * i + kind) + t + 1
                pool.wait_ge(s_ve, K)
                G.tensor_tensor(lnp[:, t, 1:2], lnp[:, t, 0:1], mhalf[:, :], ALU.pow).then_inc(s_rstd, 1)

            def gather(dst, rows, index, done, **bound):
                G.indirect_dma_start(dst, None, rows, bass.IndirectOffsetOnAxis(ap=index, axis=0), **bound).then_inc(done, 16)

            def experts(i):
                N0 = NE * i
                pool.wait_ge(s_idx, i + 1)
                pool.wait_ge(s_xd, 64 * (i + 1))
                for e in range(NE):
                    if e >= 2:
                        pool.wait_ge(xb_full, N0 + e - 1)
                    gather(xe[e % 2], x_dram[i], idx_i[:, e:e + 1], xe_full[e % 2])

            def window(i, w):
                _, loaded, step = ov[i, w][:3]
                for e in range(NE):
                    pool.wait_ge(step, OV * e + OV_ROUTE)
                    gather(xe[0], x_dram[i], idx_i[:, e:e + 1], ov[i, w][6])
                pool.wait_ge(step, OV * NE + OV_ROUTE)
                pool.wait_ge(ov[i, w][3], 16 * NE)

            def combine(i, most):
                for s in y_wr:
                    pool.wait_ge(s, 16 * (NE // 2) * (i + 1))
                def rows(t):
                    wait(pool, s_comb, NT * i + t - 1 if t >= 2 else 0)
                    for w in range(1, WINDOWS):
                        with pool.If(most > w * P):
                            for k in range(2):
                                gather(yg[t % 2][:, k, :], y_dram[i][w], pos_i[:, w, k, t:t + 1], ov[i, w][5],
                                       bounds_check=NE * P - 1, oob_is_err=False)
                            pool.wait_ge(ov[i, w][5], 32 * (t + 1))
                    for k in range(2):
                        gather(yg[t % 2][:, k, :], y_dram[i][0], pos_i[:, 0, k, t:t + 1], s_yg[t % 2],
                               bounds_check=NE * P - 1, oob_is_err=False)
                rows(0)
                rows(1)
                pool.wait_ge(s_whi, 20 + 2 * i + 1)
                hi, lo = ple_parts(i, 0)
                cs = slice(0, DC // 2)
                G.tensor_tensor(lo[:, cs, :], ple_raw(i, 0)[:, cs, :], hi[:, cs, :].bitcast(F32), ALU.subtract).then_inc(s_wlo, 1)
                for t in range(NT):
                    inverse_root(i, 1, t)
                    if t + 2 < NT:
                        rows(t + 2)

            def rope():
                for t in range(NT):
                    r = raw[t % 2].rearrange("p (h two f) -> p h two f", two=2, f=32)
                    o = rope_b.rearrange("p (h two f) -> p h two f", two=2, f=32)
                    pool.wait_ge(qkv_out, 3 * t + 3)
                    wait(pool, s_rot, t)
                    for k in range(2):
                        last = G.tensor_tensor(o[:, :, k, :], r[:, :, 1 - k, :],
                                               sin_t[:, k, t, :].unsqueeze(1).to_broadcast([P, 20, 32]), ALU.mult)
                    last.then_inc(s_ropeb, 1)

            for i in range(DEPTH):
                if i == 1:
                    rope()
                for t in range(NT):
                    inverse_root(i, 0, t)
                experts(i)
                combine(i, overflow(pool, i, window))


_INS = ["x", "p", "positions", "w_in_ab", "w_out_ab", "conv_w", "conv_b", "lru_w_r", "lru_b_r", "lru_w_i",
        "lru_b_i", "lru_lambda", "w_qkv_c", "w_out_c", "sinks_c", "ln_mix_g", "ln_mix_b", "ln_ffn_g",
        "ln_ffn_b", "w_router", "b_router", "exp_w_gate", "exp_w_up", "exp_w_down", "ple_w_proj",
        "ple_w_gate", "ple_b_gate"]


def kernel(**inputs):
    import numpy as _np
    import concourse.bacc as _bacc
    from concourse import mybir as _mybir
    from concourse.bass_utils import run_bass_kernel_spmd as _run

    nc = _bacc.Bacc("TRN2", target_bir_lowering=False, num_devices=1)
    arrays, args = {}, []
    for name in _INS:
        a = _np.ascontiguousarray(inputs[name])
        arrays[f"in_{name}_dram"] = a
        args.append(nc.dram_tensor(f"in_{name}_dram", a.shape, _mybir.dt.from_np(a.dtype), kind="ExternalInput").ap())
    args.append(nc.dram_tensor("out_0_dram", (1, S, D), _mybir.dt.float32, kind="ExternalOutput").ap())
    trunk(nc, *args)
    r = _run(nc, [arrays], core_ids=[0])
    return r.results[0]["out_0_dram"]
```
